# Optimizing a Trainium2 kernel written in Bass

```python
import math
import jax, jax.numpy as jnp
from jax import lax
import numpy as np

D_MODEL = 1024
BATCH = 1
SEQ = 512
DEPTH = 1

MEM_LEN = 256
CONV_CH = D_MODEL
CONV_K = 31
DIFF_HEADS = D_MODEL // 128
DIFF_HEAD_DIM = 64
DIFF_V_DIM = 2 * DIFF_HEAD_DIM
DIFF_WIDTH = DIFF_HEADS * DIFF_V_DIM
X_HEADS = 4
X_HEAD_DIM = D_MODEL // X_HEADS
X_WIDTH = X_HEADS * X_HEAD_DIM
N_BRANCH = 3
Q_BLOCK = 128

IN_SIZES = (
    2 * CONV_CH,
    CONV_CH,
    DIFF_WIDTH,
    DIFF_WIDTH,
    DIFF_WIDTH,
    DIFF_WIDTH,
    X_WIDTH,
    X_WIDTH,
    N_BRANCH * D_MODEL,
)
IN_COLS = sum(IN_SIZES)
IN_SPLITS = tuple(int(c) for c in np.cumsum(IN_SIZES)[:-1])


def rms_norm(x, g, eps=1e-6):
    xf = x.astype(jnp.float32)
    y = xf * lax.rsqrt(jnp.mean(xf * xf, axis=-1, keepdims=True) + eps)
    return (y * g.astype(jnp.float32)).astype(x.dtype)

def layer_norm(x, g, b, eps=1e-5):
    xf = x.astype(jnp.float32)
    mu = jnp.mean(xf, axis=-1, keepdims=True)
    xc = xf - mu
    y = xc * lax.rsqrt(jnp.mean(xc * xc, axis=-1, keepdims=True) + eps)
    return (y * g.astype(jnp.float32) + b.astype(jnp.float32)).astype(x.dtype)

def alibi_slopes(n_heads):
    return 2.0 ** (-8.0 * jnp.arange(1, n_heads + 1, dtype=jnp.float32) / n_heads)

def lambda_init_for(layer_idx):
    return 0.8 - 0.6 * math.exp(-0.3 * layer_idx)

def conformer_conv_branch(a_glu, gate, dw, dw_b, ln_g, ln_b, w_proj):
    a, b = jnp.split(a_glu, 2, axis=-1)
    u = a * jax.nn.sigmoid(b)
    u = lax.conv_general_dilated(
        u, dw[:, None, :], window_strides=(1,), padding=[(CONV_K - 1, 0)],
        dimension_numbers=("NWC", "WIO", "NWC"), feature_group_count=CONV_CH) + dw_b
    u = layer_norm(u, ln_g, ln_b)
    u = jax.nn.silu(u) * jax.nn.silu(gate)
    return u @ w_proj

def differential_attention_branch(q, k, v, gate, qn_g, kn_g, lq1, lk1, lq2, lk2,
                                  subln_g, w_proj, lambda_init):
    B, S = q.shape[0], q.shape[1]
    H, d = DIFF_HEADS, DIFF_HEAD_DIM
    nb = S // Q_BLOCK
    q = rms_norm(q.reshape(B, S, H, 2, d), qn_g)
    k = rms_norm(k.reshape(B, S, H, 2, d), kn_g)
    kt = k.transpose(0, 2, 3, 1, 4)
    vt = v.reshape(B, S, H, DIFF_V_DIM).transpose(0, 2, 1, 3)
    qb = q.reshape(B, nb, Q_BLOCK, H, 2, d).transpose(1, 0, 3, 4, 2, 5)
    lam = (jnp.exp(jnp.sum(lq1.astype(jnp.float32) * lk1.astype(jnp.float32)))
           - jnp.exp(jnp.sum(lq2.astype(jnp.float32) * lk2.astype(jnp.float32)))
           + lambda_init)
    slopes = alibi_slopes(H)
    scale = DIFF_HEAD_DIM ** -0.5
    kpos = jnp.arange(S)

    def one_block(args):
        qblk, t0 = args
        tpos = t0 + jnp.arange(Q_BLOCK)
        dist = (tpos[:, None] - kpos[None, :]).astype(jnp.float32)
        bias = -slopes[:, None, None] * dist
        s = jnp.einsum("bhmqd,bhmkd->bhmqk", qblk, kt).astype(jnp.float32) * scale
        s = s + bias[None, :, None]
        s = jnp.where(dist >= 0, s, -jnp.inf)
        p = jax.nn.softmax(s, axis=-1)
        a = (p[:, :, 0] - lam * p[:, :, 1]).astype(vt.dtype)
        return jnp.einsum("bhqk,bhkd->bhqd", a, vt)

    o = lax.map(one_block, (qb, jnp.arange(nb) * Q_BLOCK))
    o = o.transpose(1, 0, 3, 2, 4).reshape(B, S, H, DIFF_V_DIM)
    o = rms_norm(o, subln_g) * (1.0 - lambda_init)
    o = o.reshape(B, S, DIFF_WIDTH) * jax.nn.silu(gate)
    return o @ w_proj

def memory_cross_attention_branch(q, gate, mem_h, w_mem_kv, qn_g, kn_g, w_proj):
    B, S = q.shape[0], q.shape[1]
    M = mem_h.shape[1]
    k, v = jnp.split(mem_h @ w_mem_kv, 2, axis=-1)
    q = rms_norm(q.reshape(B, S, X_HEADS, X_HEAD_DIM), qn_g)
    k = rms_norm(k.reshape(B, M, X_HEADS, X_HEAD_DIM), kn_g)
    v = v.reshape(B, M, X_HEADS, X_HEAD_DIM)
    s = jnp.einsum("bshd,bmhd->bhsm", q, k).astype(jnp.float32) * (X_HEAD_DIM ** -0.5)
    p = jax.nn.softmax(s, axis=-1).astype(v.dtype)
    o = jnp.einsum("bhsm,bmhd->bshd", p, v).reshape(B, S, X_WIDTH) * jax.nn.silu(gate)
    return o @ w_proj

def first_inputs(seed: int = 0) -> dict:
    key = jax.random.key(seed)
    ks = jax.random.split(key, 24)
    f32 = jnp.float32
    L, D = DEPTH, D_MODEL

    def nrm(k, shape, scale):
        return jax.random.normal(k, shape, f32) * scale

    def gain(k, shape):
        return 1.0 + 0.05 * jax.random.normal(k, shape, f32)

    return {
        "x": jax.random.normal(ks[0], (BATCH, SEQ, D), f32),
        "mem": jax.random.normal(ks[1], (BATCH, MEM_LEN, D), f32),
        "norm_g": gain(ks[2], (L, D)),
        "mem_norm_g": gain(ks[3], (L, D)),
        "w_in": nrm(ks[4], (L, D, IN_COLS), D ** -0.5),
        "conv_dw": nrm(ks[5], (L, CONV_K, CONV_CH), CONV_K ** -0.5),
        "conv_dw_b": nrm(ks[6], (L, CONV_CH), 0.02),
        "conv_ln_g": gain(ks[7], (L, CONV_CH)),
        "conv_ln_b": nrm(ks[8], (L, CONV_CH), 0.02),
        "w_conv_proj": nrm(ks[9], (L, CONV_CH, D), CONV_CH ** -0.5),
        "diff_qn_g": gain(ks[10], (L, DIFF_HEAD_DIM)),
        "diff_kn_g": gain(ks[11], (L, DIFF_HEAD_DIM)),
        "lambda_q1": nrm(ks[12], (L, DIFF_HEAD_DIM), 0.1),
        "lambda_k1": nrm(ks[13], (L, DIFF_HEAD_DIM), 0.1),
        "lambda_q2": nrm(ks[14], (L, DIFF_HEAD_DIM), 0.1),
        "lambda_k2": nrm(ks[15], (L, DIFF_HEAD_DIM), 0.1),
        "diff_subln_g": gain(ks[16], (L, DIFF_V_DIM)),
        "w_diff_proj": nrm(ks[17], (L, DIFF_WIDTH, D), DIFF_WIDTH ** -0.5),
        "w_mem_kv": nrm(ks[18], (L, D, 2 * X_WIDTH), D ** -0.5),
        "x_qn_g": gain(ks[19], (L, X_HEAD_DIM)),
        "x_kn_g": gain(ks[20], (L, X_HEAD_DIM)),
        "w_x_proj": nrm(ks[21], (L, X_WIDTH, D), X_WIDTH ** -0.5),
        "w_out": nrm(ks[22], (L, D, D), D ** -0.5),
    }

def first_block(x, mem, norm_g, mem_norm_g, w_in, conv_dw, conv_dw_b, conv_ln_g, conv_ln_b,
              w_conv_proj, diff_qn_g, diff_kn_g, lambda_q1, lambda_k1, lambda_q2, lambda_k2,
              diff_subln_g, w_diff_proj, w_mem_kv, x_qn_g, x_kn_g, w_x_proj, w_out):
    B, S, D = x.shape
    for l in range(DEPTH):
        h = rms_norm(x, norm_g[l])
        mem_h = rms_norm(mem, mem_norm_g[l])
        (c_glu, c_gate, d_q, d_k, d_v, d_gate, x_q, x_gate, merge) = jnp.split(
            h @ w_in[l], IN_SPLITS, axis=-1)
        y_conv = conformer_conv_branch(c_glu, c_gate, conv_dw[l], conv_dw_b[l],
                                       conv_ln_g[l], conv_ln_b[l], w_conv_proj[l])
        y_diff = differential_attention_branch(
            d_q, d_k, d_v, d_gate, diff_qn_g[l], diff_kn_g[l], lambda_q1[l], lambda_k1[l],
            lambda_q2[l], lambda_k2[l], diff_subln_g[l], w_diff_proj[l], lambda_init_for(l))
        y_mem = memory_cross_attention_branch(x_q, x_gate, mem_h, w_mem_kv[l],
                                              x_qn_g[l], x_kn_g[l], w_x_proj[l])
        g = jax.nn.sigmoid(merge.reshape(B, S, N_BRANCH, D))
        y = g[:, :, 0] * y_conv + g[:, :, 1] * y_diff + g[:, :, 2] * y_mem
        x = x + y @ w_out[l]
    return x


MIX_A = D_MODEL // 2
MIX_B = D_MODEL - MIX_A
CHUNK = 128
A_GROUPS = 4
A_GROUP_DIM = MIX_A // A_GROUPS
B_HEAD_DIM = 64
B_HEADS = MIX_B // B_HEAD_DIM
LORA_W = 64
LORA_A = 64
LORA_G = 160
RWKV_COLS = 3 * MIX_B + LORA_W + LORA_A + LORA_G
IN_COLS_2 = 2 * MIX_A + RWKV_COLS
FFN_HIDDEN = ((8 * D_MODEL + 3 * 256 - 1) // (3 * 256)) * 256
ALPHA = (2 * DEPTH) ** 0.25
BETA = (8 * DEPTH) ** -0.25
LN_EPS = 1e-5
GN_EPS = 64e-5


def layer_norm_2(x, g, b, eps=LN_EPS):
    xf = x.astype(jnp.float32)
    mu = jnp.mean(xf, axis=-1, keepdims=True)
    var = jnp.mean(jnp.square(xf - mu), axis=-1, keepdims=True)
    y = (xf - mu) * lax.rsqrt(var + eps)
    return (y * g.astype(jnp.float32) + b.astype(jnp.float32)).astype(x.dtype)

def token_shift(p):
    return jnp.pad(p, ((0, 0), (1, 0), (0, 0)))[:, :-1]

def gmlp_spatial_gating(pu, pv, ln_g, ln_b, w_s, b_s):
    B, S, _ = pu.shape
    nc = S // CHUNK
    u = jax.nn.gelu(pu)
    v = layer_norm_2(jax.nn.gelu(pv), ln_g, ln_b)
    vc = v.reshape(B, nc, CHUNK, A_GROUPS, A_GROUP_DIM)
    mask = jnp.tril(jnp.ones((CHUNK, CHUNK), dtype=w_s.dtype))
    s = jnp.einsum('gts,bnsgd->bntgd', w_s * mask, vc) + b_s.T[None, None, :, :, None]
    return u * s.reshape(B, S, MIX_A)

def _rwkv7_step(S, inp):
    r, w, k, v, a, b = inp
    sa = jnp.einsum('bhij,bhj->bhi', S, a)
    S = S * w[:, :, None, :] + sa[..., None] * b[:, :, None, :] + v[..., None] * k[:, :, None, :]
    y = jnp.einsum('bhij,bhj->bhi', S, r)
    return S, y

def rwkv7_time_mix(p, mu, w0, w_up, a0, a_up, g_up, k_k, k_a, r_k, lnx_g, lnx_b):
    B, S, _ = p.shape
    p = p + (token_shift(p) - p) * mu
    r, k, v = p[..., :MIX_B], p[..., MIX_B:2 * MIX_B], p[..., 2 * MIX_B:3 * MIX_B]
    o = 3 * MIX_B
    wd = p[..., o:o + LORA_W]
    ad = p[..., o + LORA_W:o + LORA_W + LORA_A]
    gd = p[..., o + LORA_W + LORA_A:]
    f32 = jnp.float32
    wlog = -jax.nn.softplus(-(w0 + jnp.tanh(wd) @ w_up).astype(f32)) - 0.5
    decay = jnp.exp(-jnp.exp(wlog))
    a = jax.nn.sigmoid((a0 + ad @ a_up).astype(f32))
    g = jax.nn.sigmoid(gd) @ g_up
    rf, kf, vf = r.astype(f32), k.astype(f32), v.astype(f32)
    heads = lambda t: t.reshape(B, S, B_HEADS, B_HEAD_DIM)
    kk = heads(kf * k_k.astype(f32))
    kk = kk / jnp.maximum(jnp.sqrt(jnp.sum(kk * kk, axis=-1, keepdims=True)), 1e-12)
    kf = kf * (1.0 + (a - 1.0) * k_a.astype(f32))
    rh, kh, vh, wh, ah = heads(rf), heads(kf), heads(vf), heads(decay), heads(a)
    xs = tuple(jnp.swapaxes(t, 0, 1) for t in (rh, wh, kh, vh, -kk, kk * ah))
    S0 = jnp.zeros((B, B_HEADS, B_HEAD_DIM, B_HEAD_DIM), f32)
    _, y = lax.scan(_rwkv7_step, S0, xs)
    y = jnp.swapaxes(y, 0, 1)
    mu_y = jnp.mean(y, axis=-1, keepdims=True)
    var_y = jnp.mean(jnp.square(y - mu_y), axis=-1, keepdims=True)
    y = ((y - mu_y) * lax.rsqrt(var_y + GN_EPS)).reshape(B, S, MIX_B)
    y = y * lnx_g.astype(f32) + lnx_b.astype(f32)
    bonus = jnp.sum(rh * kh * r_k.astype(f32), axis=-1, keepdims=True) * vh
    y = y + bonus.reshape(B, S, MIX_B)
    return (y * g.astype(f32)).astype(p.dtype)

def second_inputs(seed: int = 0) -> dict:
    key = jax.random.key(seed)
    ks = jax.random.split(key, 32)
    L, D = DEPTH, D_MODEL
    f32 = jnp.float32
    nrm = lambda k, shape, s: jax.random.normal(k, shape, f32) * s
    return {
        "x": nrm(ks[0], (BATCH, SEQ, D), 1.0),
        "c": nrm(ks[1], (BATCH, D), 1.0),
        "emb_ln_g": 1.0 + nrm(ks[2], (D,), 0.05),
        "emb_ln_b": nrm(ks[3], (D,), 0.02),
        "w_ada": nrm(ks[4], (L, D, 6 * D), 0.5 * D ** -0.5),
        "b_ada": nrm(ks[5], (L, 6 * D), 0.02),
        "w_in": nrm(ks[6], (L, D, IN_COLS_2), D ** -0.5),
        "mu_shift": jax.random.uniform(ks[7], (L, RWKV_COLS), f32),
        "sg_ln_g": 1.0 + nrm(ks[8], (L, MIX_A), 0.05),
        "sg_ln_b": nrm(ks[9], (L, MIX_A), 0.02),
        "w_s": nrm(ks[10], (L, A_GROUPS, CHUNK, CHUNK), CHUNK ** -0.5),
        "b_s": 1.0 + nrm(ks[11], (L, A_GROUPS, CHUNK), 0.1),
        "w0": jax.random.uniform(ks[12], (L, MIX_B), f32, -6.0, 1.0),
        "w_up": nrm(ks[13], (L, LORA_W, MIX_B), LORA_W ** -0.5),
        "a0": nrm(ks[14], (L, MIX_B), 0.1),
        "a_up": nrm(ks[15], (L, LORA_A, MIX_B), LORA_A ** -0.5),
        "g_up": nrm(ks[16], (L, LORA_G, MIX_B), LORA_G ** -0.5),
        "k_k": 0.85 + nrm(ks[17], (L, MIX_B), 0.05),
        "k_a": 1.0 + nrm(ks[18], (L, MIX_B), 0.05),
        "r_k": nrm(ks[19], (L, B_HEADS, B_HEAD_DIM), 0.1),
        "lnx_g": 1.0 + nrm(ks[20], (L, MIX_B), 0.05),
        "lnx_b": nrm(ks[21], (L, MIX_B), 0.02),
        "w_out": nrm(ks[22], (L, D, D), BETA * D ** -0.5),
        "ln1_g": 1.0 + nrm(ks[23], (L, D), 0.05),
        "ln1_b": nrm(ks[24], (L, D), 0.02),
        "w_ffn_in": nrm(ks[25], (L, D, 2 * FFN_HIDDEN), D ** -0.5),
        "w_ffn_out": nrm(ks[26], (L, FFN_HIDDEN, D), BETA * FFN_HIDDEN ** -0.5),
        "ln2_g": 1.0 + nrm(ks[27], (L, D), 0.05),
        "ln2_b": nrm(ks[28], (L, D), 0.02),
    }

def second_block(x, c, emb_ln_g, emb_ln_b, w_ada, b_ada, w_in, mu_shift, sg_ln_g, sg_ln_b, w_s, b_s,
              w0, w_up, a0, a_up, g_up, k_k, k_a, r_k, lnx_g, lnx_b, w_out, ln1_g, ln1_b,
              w_ffn_in, w_ffn_out, ln2_g, ln2_b):
    x = layer_norm_2(x, emb_ln_g, emb_ln_b)
    cs = jax.nn.silu(c)
    for l in range(DEPTH):
        mod = cs @ w_ada[l] + b_ada[l]
        sh1, sc1, gt1, sh2, sc2, gt2 = [m[:, None, :] for m in jnp.split(mod, 6, axis=-1)]
        h = x * (1.0 + sc1) + sh1
        p = h @ w_in[l]
        y_a = gmlp_spatial_gating(p[..., :MIX_A], p[..., MIX_A:2 * MIX_A],
                                  sg_ln_g[l], sg_ln_b[l], w_s[l], b_s[l])
        y_b = rwkv7_time_mix(p[..., 2 * MIX_A:], mu_shift[l], w0[l], w_up[l], a0[l], a_up[l],
                             g_up[l], k_k[l], k_a[l], r_k[l], lnx_g[l], lnx_b[l])
        mix = jnp.concatenate([y_a, y_b], axis=-1) @ w_out[l]
        x = layer_norm_2(ALPHA * x + gt1 * mix, ln1_g[l], ln1_b[l])
        h = x * (1.0 + sc2) + sh2
        gu = h @ w_ffn_in[l]
        f = (jax.nn.silu(gu[..., :FFN_HIDDEN]) * gu[..., FFN_HIDDEN:]) @ w_ffn_out[l]
        x = layer_norm_2(ALPHA * x + gt2 * f, ln2_g[l], ln2_b[l])
    return x


def setup_inputs(seed=0):
    out = dict(first_inputs(seed))
    for name, value in second_inputs(seed + 1).items():
        if name != "x":
            out[name + "_2"] = value
    return out


def reference(
    x, mem, norm_g, mem_norm_g, w_in, conv_dw, conv_dw_b, conv_ln_g, conv_ln_b, w_conv_proj,
    diff_qn_g, diff_kn_g, lambda_q1, lambda_k1, lambda_q2, lambda_k2, diff_subln_g, w_diff_proj,
    w_mem_kv, x_qn_g, x_kn_g, w_x_proj, w_out, c_2, emb_ln_g_2, emb_ln_b_2, w_ada_2, b_ada_2,
    w_in_2, mu_shift_2, sg_ln_g_2, sg_ln_b_2, w_s_2, b_s_2, w0_2, w_up_2, a0_2, a_up_2, g_up_2,
    k_k_2, k_a_2, r_k_2, lnx_g_2, lnx_b_2, w_out_2, ln1_g_2, ln1_b_2, w_ffn_in_2, w_ffn_out_2,
    ln2_g_2, ln2_b_2,
):
    x = first_block(
        x, mem, norm_g, mem_norm_g, w_in, conv_dw, conv_dw_b, conv_ln_g, conv_ln_b, w_conv_proj,
        diff_qn_g, diff_kn_g, lambda_q1, lambda_k1, lambda_q2, lambda_k2, diff_subln_g,
        w_diff_proj, w_mem_kv, x_qn_g, x_kn_g, w_x_proj, w_out,
    )
    return second_block(
        x, c_2, emb_ln_g_2, emb_ln_b_2, w_ada_2, b_ada_2, w_in_2, mu_shift_2, sg_ln_g_2,
        sg_ln_b_2, w_s_2, b_s_2, w0_2, w_up_2, a0_2, a_up_2, g_up_2, k_k_2, k_a_2, r_k_2,
        lnx_g_2, lnx_b_2, w_out_2, ln1_g_2, ln1_b_2, w_ffn_in_2, w_ffn_out_2, ln2_g_2, ln2_b_2,
    )


_drawn_inputs = setup_inputs


def setup_inputs(seed=0):
    import zlib

    import numpy as np

    out = dict(_drawn_inputs(seed))
    spreads = {}
    factors = {'mem_norm_g': 8.0,
     'conv_dw_b': 7.106,
     'conv_ln_g': 5.176,
     'conv_ln_b': 31.511,
     'diff_qn_g': 4.538,
     'diff_kn_g': 4.833,
     'lambda_q1': 3.237,
     'lambda_q2': 200.0,
     'diff_subln_g': 4.407,
     'x_qn_g': 8.0,
     'x_kn_g': 8.0,
     'emb_ln_b_2': 2.793,
     'b_ada_2': 4.839,
     'sg_ln_g_2': 29.589,
     'sg_ln_b_2': 64.0,
     'b_s_2': 7.138,
     'w_up_2': 8.0,
     'a0_2': 8.0,
     'a_up_2': 3.065,
     'k_k_2': 182.474,
     'k_a_2': 8.0,
     'r_k_2': 3.428,
     'lnx_g_2': 28.423,
     'lnx_b_2': 64.0,
     'ln1_b_2': 2.82,
     'ln2_b_2': 2.905}
    for name, (base, spread) in spreads.items():
        noise = np.random.default_rng([zlib.crc32(name.encode()), seed]).standard_normal(out[name].shape)
        drawn = base * np.exp(spread * noise) if base else spread * noise
        out[name] = __import__('jax').numpy.asarray(drawn.astype(out[name].dtype))
    for name, factor in factors.items():
        out[name] = (out[name] * factor).astype(out[name].dtype)
    return out
```

```python
import math
from contextlib import ExitStack

import numpy as np

import concourse.bass as bass
from concourse import mybir

FP32 = mybir.dt.float32
FP32R = mybir.dt.float32r
ACT = mybir.ActivationFunctionType
ALU = mybir.AluOpType
AX = mybir.AxisListType.X

P = 128
D = 1024
S = 512
M = 256
KT = D // P
TT = S // P
CONV_K = 31
HEADS = 8
HALF = 64
X_HEADS = 4
X_DIM = D // X_HEADS
LAMBDA_INIT = 0.8 - 0.6 * math.exp(-0.3 * 0)
MIX = D // 2
FFN = ((8 * D + 3 * 256 - 1) // (3 * 256)) * 256
FT = FFN // P
ALPHA = 2 ** 0.25
CHUNK = 64
NC = S // CHUNK
UNIT = 1024
MASKED = -1e30

COLUMN_VECTORS = [
    ("norm_g", D), ("mem_norm_g", D), ("conv_dw_b", D), ("conv_ln_g", D), ("conv_ln_b", D),
    ("diff_qn_g", HALF), ("diff_kn_g", HALF), ("diff_subln_g", P), ("x_qn_g", X_DIM), ("x_kn_g", X_DIM),
    ("emb_ln_g_2", D), ("emb_ln_b_2", D), ("mu_shift_2", 1824), ("w0_2", MIX), ("a0_2", MIX),
    ("k_k_2", MIX), ("k_a_2", MIX), ("r_k_2", MIX), ("lnx_g_2", MIX), ("lnx_b_2", MIX),
    ("ln1_g_2", D), ("ln1_b_2", D), ("b_ada_2", 6 * D), ("c_2", D), ("conv_dw", CONV_K * D),
]
COLUMN_AT = {}
_n = 0
for _name, _size in COLUMN_VECTORS:
    COLUMN_AT[_name] = _n
    _n += -(-_size // P)
N_COLUMNS = _n

W_IN_AT = {"conv_a": 0, "conv_b": 1024, "conv_gate": 2048, "dq": 3072, "dk": 4096, "dv": 5120,
           "d_gate": 6144, "xq": 7168, "x_gate": 8192, "merge": 9216}


GATE_OF = {0: 0, 1: 2, 2: 1}


def unit_plan():
    plan = []

    def f(label, array, column):
        plan.append((label, array, "F", 0, column))

    def t(label, array, column):
        for pair in range(KT // 2):
            plan.append((f"{label}.{pair}", array, "T", 256 * pair, column))

    def project(branch, w):
        for d in range(KT):
            f(f"merge{branch}.{d}", "w_in", W_IN_AT["merge"] + GATE_OF[branch] * D + d * P)
            f(f"proj{branch}.{d}", w, d * P)

    for n in range(KT):
        f(f"conv_b.{n}", "w_in", W_IN_AT["conv_b"] + n * P)
        f(f"conv_a.{n}", "w_in", W_IN_AT["conv_a"] + n * P)
    for n in range(KT):
        f(f"conv_gate.{n}", "w_in", W_IN_AT["conv_gate"] + n * P)
    project(0, "w_conv_proj")
    for n in range(KT):
        f(f"xk.{n}", "w_mem_kv", n * P)
    for half in range(2):
        t(f"xv{half}", "w_mem_kv", D + half * 512)
    for h in range(X_HEADS):
        for c in range(2):
            f(f"xq.{2 * h + c}", "w_in", W_IN_AT["xq"] + (2 * h + c) * P)
        for c in range(2):
            f(f"x_gate.{2 * h + c}", "w_in", W_IN_AT["x_gate"] + (2 * h + c) * P)
    project(1, "w_x_proj")
    for h in range(HEADS):
        f(f"dq.{h}", "w_in", W_IN_AT["dq"] + h * P)
        f(f"dk.{h}", "w_in", W_IN_AT["dk"] + h * P)
        if h % 4 == 0:
            t(f"dv{h // 4}", "w_in", W_IN_AT["dv"] + (h // 4) * 512)
        f(f"d_gate.{h}", "w_in", W_IN_AT["d_gate"] + h * P)
    project(2, "w_diff_proj")
    for half in range(2):
        t(f"w_out{half}", "w_out", half * 512)
    for n in range(4):
        f(f"pu.{n}", "w_in_2", n * P)
    t("pv", "w_in_2", MIX)
    for n in range(14):
        f(f"rwkv.{n}", "w_in_2", 2 * MIX + n * P)
    f("rwkv.14", "w_in_2", 2 * MIX + 14 * P)
    for half in range(2):
        t(f"w_out_2{half}", "w_out_2", half * 512)
    for n in range(FT):
        f(f"ffn_g.{n}", "w_ffn_in_2", n * P)
        f(f"ffn_u.{n}", "w_ffn_in_2", FFN + n * P)
    for n in range(FT):
        plan.append((f"ffn_out.{n}", "w_ffn_out_2", "O", n * P, 0))
    return plan




class Slots:

    def __init__(self, tensors):
        self.ready = [(t, []) for t in tensors]

    def get(self, tick=None):
        while not self.ready:
            assert tick is not None, "no slot is free"
            tick()
        return self.ready.pop(0)

    def put(self, tensor, last_readers):
        self.ready.append((tensor, list(last_readers)))


class Queues:

    def __init__(self, progress):
        self.progress = progress
        self.steps = {e: [] for e in progress}
        self.count = {e: 0 for e in progress}
        self.reached = {e: {} for e in progress}

    def wait(self, engine, tokens):
        for token in tokens:
            if token is None:
                continue
            sem, value = token
            if self.reached[engine].get(sem, 0) < value:
                self.reached[engine][sem] = value
                self.steps[engine].append(lambda eng, sem=sem, value=value: eng.wait_ge(sem, value))

    def add(self, engine, make, waits, count=True):
        if engine == "pool" and self.count[engine]:
            waits = [*waits, (self.progress[engine], self.count[engine])]
        self.wait(engine, waits)
        if not count:
            self.steps[engine].append(make)
            return None
        sem = self.progress[engine]
        self.count[engine] += 1
        self.steps[engine].append(lambda eng: make(eng).then_inc(sem, 1))
        return (sem, self.count[engine])

    def latest(self):
        return [(self.progress[e], self.count[e]) for e in self.progress if self.count[e]]


def build(nc, dram, out):
    with ExitStack() as whole:
        def semaphore(name):
            return whole.enter_context(nc.semaphore(name))

        q = Queues({e: semaphore(f"{e}_progress") for e in ("pe", "act", "dve", "pool")})
        q.steps["sync"], q.reached["sync"] = [], {}

        def place(stack, name, shape, dtype=FP32):
            return stack.enter_context(nc.sbuf_tensor(name, shape, dtype))

        def pair(stack, name, shape):
            return (place(stack, name + "_hi", shape, FP32R), place(stack, name + "_lo", shape, FP32R))

        def act(o, i, func, waits, bias=0.0, scale=1.0, accum=None):
            if accum is None:
                return q.add("act", lambda e: e.activation(o, i, func, bias=bias, scale=scale), waits)
            return q.add("act", lambda e: e.activation(o, i, func, bias=bias, scale=scale, accum_out=accum), waits)

        def copy(o, i, waits):
            return act(o, i, ACT.Copy, waits)

        def tt(o, a, b, op, waits, engine="dve"):
            return q.add(engine, lambda e: e.tensor_tensor(o, a, b, op), waits)

        def ts(o, a, s1, s2, op0, op1, waits, engine="dve"):
            if op1 is None:
                return q.add(engine, lambda e: e.tensor_scalar(o, a, s1, None, op0), waits)
            return q.add(engine, lambda e: e.tensor_scalar(o, a, s1, s2, op0, op1), waits)

        def stt(o, a, s, b, op0, op1, waits):
            return q.add("dve", lambda e: e.scalar_tensor_tensor(out=o, in0=a, scalar=s, in1=b, op0=op0, op1=op1), waits)

        def dve(make, waits):
            return q.add("dve", make, waits)

        def pool(make, waits):
            return q.add("pool", make, waits)

        def mm(o, lhsT, rhs, start, stop, waits=(), signal=False):
            return q.add("pe", lambda e: e.matmul(o, lhsT, rhs, start=start, stop=stop), waits, count=signal)

        def transpose(o, i, waits, signal=False):
            ident_ap = ident[0:i.shape[0], 0:i.shape[0]]
            return q.add("pe", lambda e: e.transpose(o, i, ident_ap), waits, count=signal)

        def mm3(o, lhs, rhs, start, stop, waits=(), signal=False):
            mm(o, lhs[0], rhs[0], start, False, waits)
            mm(o, lhs[0], rhs[1], False, False)
            return mm(o, lhs[1], rhs[0], False, stop, (), signal)

        def load(o, i, sem, total, waits=()):
            q.wait("sync", waits)
            q.steps["sync"].append(lambda e: e.dma_start(o, i).then_inc(sem, 16))
            return (sem, total)

        def view(t):
            return t.bitcast(FP32)

        def split(hi, lo, value, waits):
            got_hi = copy(hi, value, waits)
            got_lo = tt(lo, value, view(hi), ALU.subtract, [*waits, got_hi])
            return [got_hi, got_lo]

        banks = [whole.enter_context(nc.psum_tensor(f"bank{n}", [P, 512], FP32)) for n in range(8)]
        unit_banks = Slots(banks[0:3])
        stat_bank = Slots(banks[3:4])
        side_banks = Slots(banks[4:8])

        RAW, SPLIT = 4, 3
        raw = [place(whole, f"raw{n}", [P, UNIT]) for n in range(RAW)]
        parts = [pair(whole, f"weight{n}", [P, UNIT]) for n in range(SPLIT)]
        ident = place(whole, "ident", [P, P])
        ones_all = place(whole, "ones_all", [P, P])
        ones_head = place(whole, "ones_head", [P, P])
        columns = place(whole, "columns", [P, N_COLUMNS])
        scratch = Slots([place(whole, f"scratch{n}", [P, S]) for n in range(7)])
        eps = place(whole, "eps", [P, 4])
        small = place(whole, "small", [P, 256])
        mod = place(whole, "mod", [P, 6, KT])

        def column(name, n=0):
            at = COLUMN_AT[name] + n
            return columns[:, at:at + 1]

        small_at = [0]

        def small_columns(n=1):
            at = small_at[0]
            if at + n > 256:
                at = 0
            small_at[0] = at + n
            return small[:, at:at + n]

        sem_columns = semaphore("columns_loaded")
        columns_ready = load(columns[:, :], dram["columns"], sem_columns, 16)
        pool(lambda e: e.memset(ident[:, :], 0.0), [])
        pool(lambda e: e.memset(ones_all[:, :], 1.0), [])
        zeroed = pool(lambda e: e.memset(ones_head[:, :], 0.0), [])
        pool(lambda e: e.memset(eps[:, 0:1], 1e-6), [])
        pool(lambda e: e.memset(eps[:, 1:2], 1e-5), [])
        pool(lambda e: e.memset(eps[:, 2:3], 64e-5), [])
        pool(lambda e: e.memset(eps[:, 3:4], 0.0), [])
        pool(lambda e: e.memset(ones_head[0:HALF, 0:HALF], 1.0), [zeroed])
        cleared = pool(lambda e: e.memset(ones_head[HALF:P, HALF:P], 1.0), [])
        consts_ready = pool(lambda e: e.affine_select(
            out=ident[:, :], in_=ident[:, :], pattern=[[-1, P]], compare_op=ALU.not_equal, fill=1.0,
            base=0, channel_multiplier=1), [cleared])
        for engine in ("pe", "act", "dve"):
            q.wait(engine, [consts_ready, columns_ready])
        q.wait("pool", [columns_ready, consts_ready])
        EPS6, EPS5, EPSG = eps[:, 0:1], eps[:, 1:2], eps[:, 2:3]

        tasks = []

        def spawn(generator):
            tasks.append(generator)
            return generator

        def advance(task):
            try:
                next(task)
            except StopIteration:
                tasks.remove(task)

        def tick():
            for task in list(tasks):
                if task in tasks:
                    advance(task)

        def finish(task):
            while task in tasks:
                tick()

        def finish_all():
            while tasks:
                tick()

        plan = unit_plan()
        raw_sems = [semaphore(f"raw{n}_loaded") for n in range(RAW)]
        raw_free = [[] for _ in range(RAW)]
        part_free = [[] for _ in range(SPLIT)]
        part_ready = {}
        raw_ready = {}
        taken = [0]

        def load_unit(u):
            if u < len(plan):
                n = u % RAW
                raw_ready[u] = load(raw[n][:, :], dram["weights"][u], raw_sems[n], 16 * (u // RAW + 1), raw_free[n])

        def split_unit(u):
            if u < len(plan):
                n, hi, lo = u % RAW, *parts[u % SPLIT]
                part_ready[u] = split(hi[:, :], lo[:, :], raw[n][:, :], [raw_ready[u], *part_free[u % SPLIT]])
                raw_free[n] = part_ready[u]
                load_unit(u + RAW)

        for u in range(RAW):
            load_unit(u)

        def start_weights():
            for u in range(SPLIT):
                split_unit(u)

        def take(label):
            u = taken[0]
            assert plan[u][0] == label, (plan[u][0], label)
            taken[0] += 1
            return u, parts[u % SPLIT], part_ready[u]

        def give_back(u, last_product):
            part_free[u % SPLIT] = [last_product]
            split_unit(u + SPLIT)

        def feature_unit(label, x, width=S, waits=()):
            u, (hi, lo), ready = take(label)
            bank, free = unit_banks.get(tick)
            for k in range(KT):
                cols = slice(k * P, (k + 1) * P)
                done = mm3(bank[:, 0:width], (hi[:, cols], lo[:, cols]), (x[0][:, k, 0:width], x[1][:, k, 0:width]),
                           k == 0, k == KT - 1, [*ready, *free, *waits] if k == 0 else (), signal=k == KT - 1)
                if k == KT // 2 - 1:
                    tick()
            give_back(u, done)
            tick()
            return bank, done

        def token_units(label, x, tiles, out_banks, frees, waits=()):
            done = None
            for n in range(KT // 2):
                u, (hi, lo), ready = take(f"{label}.{n}")
                for t in range(tiles):
                    tok = slice(t * P, (t + 1) * P)
                    for j in range(2):
                        k = 2 * n + j
                        cols = slice(j * 512, (j + 1) * 512)
                        last = n == KT // 2 - 1 and j == 1
                        done = mm3(out_banks[t][:, :], (x[0][:, k, tok], x[1][:, k, tok]), (hi[:, cols], lo[:, cols]),
                                   k == 0, last, [*ready, *frees[t], *waits] if j == 0 else (),
                                   signal=last or (t == tiles - 1 and j == 1))
                        if last:
                            tile_done[t] = done
                    if t == tiles // 2 - 1:
                        tick()
                give_back(u, done)
                tick()
            return list(tile_done[:tiles])

        tile_done = [None] * TT

        def rsqrt_rows(source, waits, n, bias, width=S):
            r, free = scratch.get()
            got_ln = act(r[:, 0:width], source, ACT.Ln, [*waits, *free], bias=bias, scale=1.0 / n)
            got = act(r[:, 0:width], r[:, 0:width], ACT.Exp, [got_ln], scale=-0.5)
            return r, got_ln, got

        def rsqrt_column(o, i, scale, bias, waits):
            t = small_columns()
            got_ln = act(t, i, ACT.Ln, waits, bias=bias, scale=scale)
            return act(o, t, ACT.Exp, [got_ln], scale=-0.5)

        def turn_scaled(source, ready, hi, lo, gains, tiles, free, shifts=None):
            tokens = []
            for k in range(KT):
                bank, bank_free = side_banks.get()
                width = tiles * P
                for t in range(tiles):
                    turned = transpose(bank[:, t * P:(t + 1) * P], source[t][:, k * P:(k + 1) * P],
                                       [*ready[t], *bank_free], signal=t == tiles - 1)
                full, scratch_free = scratch.get()
                if shifts is None:
                    got = ts(full[:, 0:width], bank[:, 0:width], gains(k), None, ALU.mult, None, [turned, *scratch_free])
                else:
                    got = ts(full[:, 0:width], bank[:, 0:width], gains(k), shifts(k), ALU.mult, ALU.add,
                             [turned, *scratch_free])
                side_banks.put(bank, [got])
                both = split(hi[:, k, 0:width], lo[:, k, 0:width], full[:, 0:width], [got, *free])
                scratch.put(full, both)
                tokens += both
            return tokens[-2:]

        y_T = place(whole, "y_T", [P, KT, S])
        x_rows = [y_T[:, 2 * t:2 * t + 2, :].rearrange("p a b -> p (a b)") for t in range(TT)]
        branch = pair(whole, "branch", [P, KT, S])
        first = ExitStack()
        h_T = pair(first, "h_T", [P, KT, S])

        ada = [place(first, f"ada{n}", [P, D]) for n in range(2)]
        ada_sum = place(first, "ada_sum", [P, D])
        silu_c = place(first, "silu_c", [P, KT])
        ada_sems = [semaphore(f"ada{n}_loaded") for n in range(2)]
        ada_count = [0]
        ada_free = [[], []]
        silu_ready = act(silu_c[:, :], columns[:, COLUMN_AT["c_2"]:COLUMN_AT["c_2"] + KT], ACT.Silu, [])

        def modulation_vector(v, result_free):
            got = None
            for k in range(KT):
                n = ada_count[0]
                ada_count[0] += 1
                s = n % 2
                loaded = load(ada[s][:, :], dram["w_ada"][k * P:(k + 1) * P, v * D:(v + 1) * D], ada_sems[s],
                              16 * (n // 2 + 1), ada_free[s])
                if k == 0:
                    got = ts(ada_sum[:, :], ada[s][:, :], silu_c[:, 0:1], None, ALU.mult, None,
                             [loaded, silu_ready, *result_free], engine="pool")
                else:
                    scaled = ts(ada[s][:, :], ada[s][:, :], silu_c[:, k:k + 1], None, ALU.mult, None,
                                [loaded, silu_ready], engine="pool")
                    got = tt(ada_sum[:, :], ada_sum[:, :], ada[s][:, :], ALU.add, [scaled, got], engine="pool")
                ada_free[s] = [got]
                yield
            vector_sum[0] = got

        vector_sum = [None]
        mod_ready = {}

        def modulation_columns():
            free = []
            for v in range(6):
                yield from modulation_vector(v, free)
                for _ in range(4):
                    yield
                bank, bank_free = stat_bank.get()
                for k in range(KT):
                    summed = mm(bank[:, k:k + 1], ada_sum[:, k * P:(k + 1) * P], ones_all[:, 0:1], True, True,
                                [vector_sum[0], *bank_free] if k == 0 else (), signal=k == KT - 1)
                at = COLUMN_AT["b_ada_2"] + v * KT
                mod_ready[v] = tt(mod[:, v, :], bank[:, 0:KT], columns[:, at:at + KT], ALU.add, [summed])
                stat_bank.put(bank, [mod_ready[v]])
                free = [summed]

        def rms_rows(source, sem, rows_loaded, count, stack, name):
            tiles = [place(stack, f"{name}{t}", [P, D]) for t in range(count)]
            ready = []
            for t in range(count):
                loaded = load(tiles[t][:, :], source[t * P:(t + 1) * P, :], sem, rows_loaded + 16 * (t + 1))
                loads.append(loaded)
            for t in range(count):
                sq, free = scratch.get()
                squares, total = small_columns(2), small_columns()
                waits = [loads[-1], *free]
                got = act(sq[:, :], tiles[t][:, 0:512], ACT.Square, waits, accum=squares[:, 0:1])
                got = act(sq[:, :], tiles[t][:, 512:1024], ACT.Square, [got], accum=squares[:, 1:2])
                scratch.put(sq, [got])
                summed = tt(total, squares[:, 0:1], squares[:, 1:2], ALU.add, [got])
                r = small_columns()
                got = rsqrt_column(r, total, 1.0 / D, EPS6, [summed])
                ready.append([ts(tiles[t][:, :], tiles[t][:, :], r, None, ALU.mult, None, [got])])
            return tiles, ready

        loads = []
        sem_x = semaphore("x_loaded")
        with ExitStack() as phase:
            tiles, ready = rms_rows(dram["x"], sem_x, 0, TT, phase, "x_rows")
            start_weights()
            h_ready = turn_scaled(tiles, ready, *h_T, lambda k: column("norm_g", k), TT, [])
        fence = q.latest()

        ada_task = spawn(modulation_columns())

        def project(n, y_first, waits):
            for d in range(KT):
                bank, done = feature_unit(f"merge{n}.{d}", h_T)
                gate, free = scratch.get(tick)
                gated = act(gate[:, :], bank[:, :], ACT.Sigmoid, [done, *free])
                unit_banks.put(bank, [gated])
                bank, done = feature_unit(f"proj{n}.{d}", branch, waits=waits if d == 0 else ())
                if y_first:
                    y_last[d] = tt(y_T[:, d, :], bank[:, :], gate[:, :], ALU.mult, [done, gated])
                    unit_banks.put(bank, [y_last[d]])
                else:
                    product = tt(gate[:, :], bank[:, :], gate[:, :], ALU.mult, [done, gated])
                    unit_banks.put(bank, [product])
                    y_last[d] = tt(y_T[:, d, :], y_T[:, d, :], gate[:, :], ALU.add, [product, y_last[d]])
                scratch.put(gate, [y_last[d]])
            return done

        y_last = [None] * KT
        branch_free = []

        with ExitStack() as phase:
            PAD = CONV_K - 1
            padded = [place(phase, f"conv_in{n}", [P, PAD + S]) for n in range(2)]
            conv = place(phase, "conv_out", [P, KT, S])
            pads = [pool(lambda e, n=n: e.memset(padded[n][:, 0:PAD], 0.0), fence) for n in range(2)]
            q.wait("dve", fence)
            padded_slots = Slots(padded)
            conv_ready = [None] * KT

            def taps(n, u, ready):
                weight = lambda j: columns[:, COLUMN_AT["conv_dw"] + j * KT + n:COLUMN_AT["conv_dw"] + j * KT + n + 1]
                got = ts(conv[:, n, :], u[:, 0:S], weight(0), column("conv_dw_b", n), ALU.mult, ALU.add, [ready])
                for j in range(1, CONV_K):
                    got = stt(conv[:, n, :], u[:, j:j + S], weight(j), conv[:, n, :], ALU.mult, ALU.add, [got])
                    if j % 8 == 7:
                        yield
                conv_ready[n] = got
                padded_slots.put(u, [got])

            for n in range(KT):
                bank_b, done_b = feature_unit(f"conv_b.{n}", h_T, waits=h_ready)
                gate, free = scratch.get(tick)
                gated = act(gate[:, :], bank_b[:, :], ACT.Sigmoid, [done_b, *free])
                unit_banks.put(bank_b, [gated])
                bank_a, done_a = feature_unit(f"conv_a.{n}", h_T)
                u, free = padded_slots.get(tick)
                got = tt(u[:, PAD:PAD + S], bank_a[:, :], gate[:, :], ALU.mult, [done_a, gated, *free, *pads])
                unit_banks.put(bank_a, [got])
                scratch.put(gate, [got])
                spawn(taps(n, u, got))

            def conv_norm():
                while None in conv_ready:
                    yield
                bank, free = stat_bank.get()
                for n in range(KT):
                    summed = mm(bank[:, :], ones_all[:, :], conv[:, n, :], n == 0, n == KT - 1,
                                [conv_ready[n], *free], signal=n == KT - 1)
                centred = []
                for n in range(KT):
                    centred.append(stt(conv[:, n, :], bank[:, :], -1.0 / D, conv[:, n, :], ALU.mult, ALU.add, [summed]))
                stat_bank.put(bank, [centred[-1]])
                bank, free = side_banks.get()
                for n in range(KT):
                    sq, sq_free = scratch.get()
                    squared = act(sq[:, :], conv[:, n, :], ACT.Square, [centred[n], *sq_free])
                    summed = mm(bank[:, :], ones_all[:, :], sq[:, :], n == 0, n == KT - 1, [squared, *free], signal=True)
                    scratch.put(sq, [summed])
                r, got_ln, got = rsqrt_rows(bank[:, :], [summed], D, EPS5)
                side_banks.put(bank, [got_ln])
                for n in range(KT):
                    conv_ready[n] = tt(conv[:, n, :], conv[:, n, :], r[:, :], ALU.mult, [got, centred[n]])
                scratch.put(r, [conv_ready[-1]])

            finish_all_but = [t for t in tasks if t is not ada_task]
            for task in finish_all_but:
                finish(task)
            norm_task = spawn(conv_norm())
            branch_ready = []
            for n in range(KT):
                bank, done = feature_unit(f"conv_gate.{n}", h_T)
                finish(norm_task)
                normed, free = scratch.get(tick)
                got = act(normed[:, :], conv[:, n, :], ACT.Silu, [conv_ready[n], *free], bias=column("conv_ln_b", n),
                          scale=column("conv_ln_g", n))
                gate, free = scratch.get(tick)
                gated = act(gate[:, :], bank[:, :], ACT.Silu, [done, *free])
                unit_banks.put(bank, [gated])
                got = tt(normed[:, :], normed[:, :], gate[:, :], ALU.mult, [got, gated])
                scratch.put(gate, [got])
                both = split(branch[0][:, n, :], branch[1][:, n, :], normed[:, :], [got])
                scratch.put(normed, both)
                branch_ready += both
            last_product = project(0, True, branch_ready[-2:])
            branch_free = [last_product]
        fence = q.latest()

        with ExitStack() as phase:
            k_x = pair(phase, "k_x", [P, KT, M])
            v_x = pair(phase, "v_x", [P, M // P, D])
            for engine in ("act", "dve", "pe"):
                q.wait(engine, fence)
            with ExitStack() as inner:
                mem_T = pair(inner, "mem_T", [P, KT, M])
                with ExitStack() as rows:
                    q.wait("sync", fence)
                    tiles, ready = rms_rows(dram["mem"], sem_x, 16 * TT, M // P, rows, "mem_rows")
                    mem_ready = turn_scaled(tiles, ready, *mem_T, lambda k: column("mem_norm_g", k), M // P, [])

                def finish_norm(parts_in, ones, size, gains, outs, width, record, out_free=()):
                    squares = []
                    for bank, done in parts_in:
                        sq, free = scratch.get()
                        squares.append((sq, act(sq[:, 0:width], bank[:, 0:width], ACT.Square, [done, *free])))
                    yield
                    stat, free = stat_bank.get()
                    for n, (sq, squared) in enumerate(squares):
                        summed = mm(stat[:, 0:width], ones[:, :], sq[:, 0:width], n == 0, n == len(squares) - 1,
                                    [squared, *free], signal=True)
                        scratch.put(sq, [summed])
                    r, got_ln, got = rsqrt_rows(stat[:, 0:width], [summed], size, EPS6, width)
                    stat_bank.put(stat, [got_ln])
                    full, free = scratch.get()
                    for (bank, done), gain, (hi, lo) in zip(parts_in, gains, outs):
                        scaled = stt(full[:, 0:width], bank[:, 0:width], gain, r[:, 0:width], ALU.mult, ALU.mult,
                                     [got, *free])
                        unit_banks.put(bank, [scaled])
                        both = split(hi, lo, full[:, 0:width], [scaled, *out_free])
                        free = both
                        record += both
                    scratch.put(r, [scaled])
                    scratch.put(full, both)

                k_tokens = []
                task = None
                for h in range(X_HEADS):
                    held = []
                    for c in range(2):
                        held.append(feature_unit(f"xk.{2 * h + c}", mem_T, width=M, waits=mem_ready))
                    if task is not None:
                        finish(task)
                    task = spawn(finish_norm(held, ones_all, X_DIM, [column("x_kn_g", c) for c in range(2)],
                                             [(k_x[0][:, 2 * h + c, :], k_x[1][:, 2 * h + c, :]) for c in range(2)],
                                             M, k_tokens))
                    tick()
                v_tokens = []
                finish(task)
                for half in range(2):
                    held = [side_banks.get() for _ in range(M // P)]
                    done = token_units(f"xv{half}", mem_T, M // P, [b for b, _ in held], [f for _, f in held])
                    cols = slice(half * 512, (half + 1) * 512)
                    for t, (bank, _) in enumerate(held):
                        both = split(v_x[0][:, t, cols], v_x[1][:, t, cols], bank[:, :], [done[t]])
                        side_banks.put(bank, both)
                        v_tokens += both
                inner_fence = q.latest()

            q_x = [pair(phase, f"q_x{n}", [P, 2, S]) for n in range(2)]
            p_T = pair(phase, "p_T", [P, M // P, S])
            for engine in ("act", "dve", "pe"):
                q.wait(engine, inner_fence)
            x_gain = place(phase, "x_gain", [P, 2])
            x_gain_ready = ts(x_gain[:, :], columns[:, COLUMN_AT["x_qn_g"]:COLUMN_AT["x_qn_g"] + 2], X_DIM ** -0.5, None,
                              ALU.mult, None, [])
            q.wait("dve", [x_gain_ready])
            q_free = [[], []]
            p_T_free = []

            def cross_attention(h, q_pair, q_tokens, gates):
                nonlocal p_T_free
                p_tokens = []
                held = None
                for t in range(TT + 1):
                    if t < TT:
                        scores, free = side_banks.get()
                        for c in range(2):
                            qs = slice(t * P, (t + 1) * P)
                            done = mm3(scores[:, 0:M], (q_pair[0][:, c, qs], q_pair[1][:, c, qs]),
                                       (k_x[0][:, 2 * h + c, :], k_x[1][:, 2 * h + c, :]), c == 0, c == 1,
                                       [*q_tokens, *k_tokens, *free], signal=c == 1)
                        top, total, inverse = small_columns(), small_columns(), small_columns()
                        got = dve(lambda e, top=top, scores=scores: e.tensor_reduce(
                            top, scores[:, 0:M], AX, ALU.max, negate=True), [done])
                        p, free = scratch.get()
                        got = act(p[:, 0:M], scores[:, 0:M], ACT.Exp, [got, *free], bias=top, accum=total)
                        side_banks.put(scores, [got])
                        got = dve(lambda e, inverse=inverse, total=total: e.reciprocal(inverse, total), [got])
                        ready = ts(p[:, 0:M], p[:, 0:M], inverse, None, ALU.mult, None, [got])
                    if held is not None:
                        turned, free = side_banks.get()
                        before, before_ready, u = held
                        for j in range(M // P):
                            done = transpose(turned[:, j * P:(j + 1) * P], before[:, j * P:(j + 1) * P],
                                             [before_ready, *free], signal=j == M // P - 1)
                        scratch.put(before, [done])
                        qs = slice(u * P, (u + 1) * P)
                        grid = turned[:, 0:M].rearrange("p (j c) -> p j c", c=P)
                        both = split(p_T[0][:, :, qs], p_T[1][:, :, qs], grid, [done, *p_T_free])
                        side_banks.put(turned, both)
                        p_tokens += both
                    held = (p, ready, t) if t < TT else None
                    yield
                q_free[h % 2] = [done]
                for c in range(2):
                    o, free = side_banks.get()
                    for j in range(M // P):
                        cols = slice(h * X_DIM + c * P, h * X_DIM + (c + 1) * P)
                        done = mm3(o[:, :], (v_x[0][:, j, cols], v_x[1][:, j, cols]), (p_T[0][:, j, :], p_T[1][:, j, :]),
                                   j == 0, j == M // P - 1, [*p_tokens, *v_tokens, *free], signal=j == M // P - 1)
                    p_T_free = [done]
                    while gates[c] is None:
                        yield
                    gate, gated = gates[c]
                    got = tt(gate[:, :], o[:, :], gate[:, :], ALU.mult, [done, gated])
                    side_banks.put(o, [got])
                    both = split(branch[0][:, 2 * h + c, :], branch[1][:, 2 * h + c, :], gate[:, :], [got, *branch_free])
                    scratch.put(gate, both)
                    branch_tokens.extend(both)
                    yield

            branch_tokens = []
            task = None
            for h in range(X_HEADS):
                held = [feature_unit(f"xq.{2 * h + c}", h_T) for c in range(2)]
                q_tokens = []
                gains = [x_gain[:, c:c + 1] for c in range(2)]
                norm = spawn(finish_norm(held, ones_all, X_DIM, gains,
                                         [(q_x[h % 2][0][:, c, :], q_x[h % 2][1][:, c, :]) for c in range(2)],
                                         S, q_tokens, q_free[h % 2]))
                tick()
                gates = [None, None]
                for c in range(2):
                    bank, done = feature_unit(f"x_gate.{2 * h + c}", h_T)
                    gate, free = scratch.get(tick)
                    gated = act(gate[:, :], bank[:, :], ACT.Silu, [done, *free])
                    unit_banks.put(bank, [gated])
                    gates[c] = (gate, gated)
                finish(norm)
                if task is not None:
                    finish(task)
                task = spawn(cross_attention(h, q_x[h % 2], q_tokens, gates))
            finish(task)
            branch_free = [project(1, False, branch_tokens[-2:])]
        fence = q.latest()

        with ExitStack() as phase:
            distance = place(phase, "distance", [P, S])
            bias = [place(phase, f"bias{n}", [P, S]) for n in range(2)]
            q_d = [pair(phase, f"q_d{n}", [P, S]) for n in range(2)]
            k_d = [pair(phase, f"k_d{n}", [P, S]) for n in range(2)]
            v_d = pair(phase, "v_d", [P, TT, 512])
            a_T = [pair(phase, f"a_T{j}_", [P, S - j * P]) for j in range(TT)]
            lam_in = place(phase, "lam_in", [P, 4, HALF])
            lam = place(phase, "lam", [P, 8])
            for engine in ("act", "dve", "pe", "pool"):
                q.wait(engine, fence)
            sem_lam = semaphore("lambda_loaded")
            for n, name in enumerate(("lambda_q1", "lambda_k1", "lambda_q2", "lambda_k2")):
                loaded = load(lam_in[:, n, :], dram[name].broadcast_to([P, HALF]), sem_lam, 16 * (n + 1), fence)
            for n in range(2):
                got = tt(lam_in[:, 2 * n, :], lam_in[:, 2 * n, :], lam_in[:, 2 * n + 1, :], ALU.mult, [loaded])
                got = dve(lambda e, n=n: e.tensor_reduce(lam[:, n:n + 1], lam_in[:, 2 * n, :], AX, ALU.add), [got])
            got = act(lam[:, 2:4], lam[:, 0:2], ACT.Exp, [got])
            got = tt(lam[:, 4:5], lam[:, 3:4], lam[:, 2:3], ALU.subtract, [got])
            minus_lam_ready = ts(lam[:, 5:6], lam[:, 4:5], -LAMBDA_INIT, None, ALU.add, None, [got])
            minus_lam = lam[:, 5:6]
            got = pool(lambda e: e.iota(distance[:, :], pattern=[[1, S]], base=-(S - P), channel_multiplier=-1,
                                        allow_small_or_imprecise_dtypes=True), [])
            distance_ready = pool(lambda e: e.affine_select(
                out=distance[:, :], in_=distance[:, :], pattern=[[-1, S]], compare_op=ALU.is_ge, fill=MASKED,
                base=S - P, channel_multiplier=1), [got])
            q_gain = lam[:, 6:7]
            o_gain = lam[:, 7:8]
            ts(q_gain, column("diff_qn_g"), HALF ** -0.5, None, ALU.mult, None, [])
            gains_ready = ts(o_gain, column("diff_subln_g"), 1.0 - LAMBDA_INIT, None, ALU.mult, None, [])
            q.wait("dve", [gains_ready])
            bias_free = [[], []]
            qk_free = [[], []]
            a_T_free = []
            v_free = []
            v_tokens = []
            branch_tokens = []

            def differential_attention(h, qk_tokens, gate_box, v_waits):
                nonlocal a_T_free, v_free
                (q_hi, q_lo), (k_hi, k_lo) = q_d[h % 2], k_d[h % 2]
                slope = 2.0 ** (-8.0 * (h + 1) / HEADS)
                biased = ts(bias[h % 2][:, :], distance[:, :], slope, None, ALU.mult, None,
                            [distance_ready, *bias_free[h % 2]], engine="pool")
                a_tokens = []
                held = None
                for t in range(TT + 1):
                    if t < TT:
                        n = (t + 1) * P
                        qs = slice(t * P, (t + 1) * P)
                        tops, totals, inverse = small_columns(2), small_columns(2), small_columns(2)
                        ps = []
                        for m in range(2):
                            rows = slice(m * HALF, (m + 1) * HALF)
                            scores, free = side_banks.get()
                            done = mm3(scores[:, 0:n], (q_hi[rows, qs], q_lo[rows, qs]), (k_hi[rows, 0:n], k_lo[rows, 0:n]),
                                       True, True, [*qk_tokens, *free], signal=True)
                            s, free = scratch.get()
                            got = dve(lambda e, s=s, scores=scores, m=m, n=n, tops=tops: e.tensor_tensor_reduce(
                                out=s[:, 0:n], in0=scores[:, 0:n], in1=bias[h % 2][:, S - n:S], scale=1.0,
                                scalar=MASKED, op0=ALU.add, op1=ALU.max, accum_out=tops[:, m:m + 1]),
                                [done, biased, *free])
                            side_banks.put(scores, [got])
                            ps.append((s, got))
                        minus = small_columns(2)
                        got = ts(minus, tops, -1.0, None, ALU.mult, None, [got])
                        for m in range(2):
                            s, _ = ps[m]
                            done_exp = act(s[:, 0:n], s[:, 0:n], ACT.Exp, [got], bias=minus[:, m:m + 1],
                                           accum=totals[:, m:m + 1])
                        got = dve(lambda e, inverse=inverse, totals=totals: e.reciprocal(inverse, totals), [done_exp])
                        second = small_columns()
                        c1 = ts(second, inverse[:, 1:2], minus_lam, None, ALU.mult, None, [got, minus_lam_ready])
                        (s0, _), (s1, _) = ps
                        got = ts(s0[:, 0:n], s0[:, 0:n], inverse[:, 0:1], None, ALU.mult, None, [got])
                        ready = stt(s0[:, 0:n], s1[:, 0:n], second, s0[:, 0:n], ALU.mult, ALU.add, [got, c1])
                        scratch.put(s1, [ready])
                    if held is not None:
                        before, before_ready, u = held
                        turned, free = side_banks.get()
                        for j in range(u + 1):
                            done = transpose(turned[:, j * P:(j + 1) * P], before[:, j * P:(j + 1) * P],
                                             [before_ready, *free], signal=j == u)
                        scratch.put(before, [done])
                        cols = [slice((u - j) * P, (u - j + 1) * P) for j in range(u + 1)]
                        for j in range(u + 1):
                            got = copy(a_T[j][0][:, cols[j]], turned[:, j * P:(j + 1) * P], [done, *a_T_free])
                        for j in range(u + 1):
                            both = [got, tt(a_T[j][1][:, cols[j]], turned[:, j * P:(j + 1) * P],
                                            view(a_T[j][0][:, cols[j]]), ALU.subtract, [got])]
                        side_banks.put(turned, both)
                        a_tokens += both
                    held = (s0, ready, t) if t < TT else None
                    yield
                bias_free[h % 2] = [ready]
                qk_free[h % 2] = [done]
                o, free = side_banks.get()
                cols = slice((h % 4) * P, (h % 4 + 1) * P)
                for j in range(TT):
                    done = mm3(o[:, j * P:S], (v_d[0][:, j, cols], v_d[1][:, j, cols]), (a_T[j][0][:, :], a_T[j][1][:, :]),
                               j == 0, j == TT - 1, [*a_tokens, *v_waits, *free], signal=j == TT - 1)
                a_T_free = [done]
                v_free = [done]
                sq, free = scratch.get()
                squared = act(sq[:, :], o[:, :], ACT.Square, [done, *free])
                yield
                stat, free = stat_bank.get()
                summed = mm(stat[:, :], ones_all[:, :], sq[:, :], True, True, [squared, *free], signal=True)
                scratch.put(sq, [summed])
                r, got_ln, got = rsqrt_rows(stat[:, :], [summed], P, EPS6)
                stat_bank.put(stat, [got_ln])
                while gate_box[0] is None:
                    yield
                gate, gated = gate_box[0]
                got = stt(r[:, :], o[:, :], o_gain, r[:, :], ALU.mult, ALU.mult, [got])
                side_banks.put(o, [got])
                got = tt(gate[:, :], gate[:, :], r[:, :], ALU.mult, [got, gated])
                scratch.put(r, [got])
                both = split(branch[0][:, h, :], branch[1][:, h, :], gate[:, :], [got, *branch_free])
                scratch.put(gate, both)
                branch_tokens.extend(both)

            def norm_qk(bank, done, gain, hi, lo, record, free):
                yield from finish_norm([(bank, done)], ones_head, HALF, [gain], [(hi, lo)], S, record, free)

            attention = None
            for h in range(HEADS):
                qk_tokens = []
                bank, done = feature_unit(f"dq.{h}", h_T)
                norm_q = spawn(norm_qk(bank, done, q_gain, q_d[h % 2][0][:, :], q_d[h % 2][1][:, :], qk_tokens,
                                       qk_free[h % 2]))
                bank, done = feature_unit(f"dk.{h}", h_T)
                norm_k = spawn(norm_qk(bank, done, column("diff_kn_g"), k_d[h % 2][0][:, :], k_d[h % 2][1][:, :],
                                       qk_tokens, qk_free[h % 2]))
                tick()
                if h % 4 == 0:
                    if attention is not None:
                        finish(attention)
                    held = [side_banks.get() for _ in range(TT)]
                    done = token_units(f"dv{h // 4}", h_T, TT, [b for b, _ in held], [f for _, f in held])
                    v_tokens = []
                    for t, (bank, _) in enumerate(held):
                        both = split(v_d[0][:, t, :], v_d[1][:, t, :], bank[:, :], [done[t], *v_free])
                        side_banks.put(bank, both)
                        v_tokens += both
                gate_box = [None]
                finish(norm_q)
                finish(norm_k)
                if attention is not None:
                    finish(attention)
                attention = spawn(differential_attention(h, qk_tokens, gate_box, v_tokens))
                bank, done = feature_unit(f"d_gate.{h}", h_T)
                gate, free = scratch.get(tick)
                gated = act(gate[:, :], bank[:, :], ACT.Silu, [done, *free])
                unit_banks.put(bank, [gated])
                gate_box[0] = (gate, gated)
            finish(attention)
            last = project(2, False, branch_tokens[-2:])
        finish_all()

        y_tokens = []
        for d in range(KT):
            y_tokens += split(h_T[0][:, d, :], h_T[1][:, d, :], y_T[:, d, :], [y_last[d], last])
        sem_res = semaphore("x_again_loaded")
        for t in range(TT):
            loaded = load(x_rows[t], dram["x"][t * P:(t + 1) * P, :], sem_res, 16 * (t + 1), y_tokens[-2:])
        x_ready = [None] * TT

        def token_projection(label, x, waits, consume):
            for half in range(2):
                held = [side_banks.get(tick) for _ in range(TT)]
                done = token_units(f"{label}{half}", x, TT, [b for b, _ in held], [f for _, f in held], waits=waits)
                for t, (bank, _) in enumerate(held):
                    side_banks.put(bank, [consume(t, slice(half * 512, (half + 1) * 512), bank, done[t])])

        def add_residual(t, cols, bank, done):
            x_ready[t] = tt(x_rows[t][:, cols], x_rows[t][:, cols], bank[:, :], ALU.add, [done, loaded])
            return x_ready[t]

        token_projection("w_out", h_T, y_tokens[-2:], add_residual)
        first.close()
        fence = q.latest()

        fold = place(whole, "fold", [P, 4, KT])
        one_minus_ka = place(whole, "one_minus_ka", [P, MIX // P])
        for engine in ("act", "dve", "pe", "pool"):
            q.wait(engine, fence)

        def vector_columns(name, n=KT):
            return columns[:, COLUMN_AT[name]:COLUMN_AT[name] + n]

        def fold_modulation(n, gain, shift, shift_v, scale_v):
            g, b = fold[:, 2 * n, :], fold[:, 2 * n + 1, :]
            got = stt(g, mod[:, scale_v, :], 1.0, vector_columns(gain), ALU.add, ALU.mult, [mod_ready[scale_v]])
            got = stt(b, mod[:, scale_v, :], 1.0, vector_columns(shift), ALU.add, ALU.mult, [mod_ready[scale_v]])
            return tt(b, b, mod[:, shift_v, :], ALU.add, [got, mod_ready[shift_v]])

        folded = [fold_modulation(0, "emb_ln_g_2", "emb_ln_b_2", 0, 1), fold_modulation(1, "ln1_g_2", "ln1_b_2", 3, 4)]
        ts(one_minus_ka[:, :], vector_columns("k_a_2", MIX // P), -1.0, 1.0, ALU.mult, ALU.add, [])

        def normalise_rows(rows, width, eps_column, waits, out=None):
            pieces = width // 512
            stats = small_columns(6 * pieces)
            for n in range(pieces):
                got = dve(lambda e, n=n: e.bn_stats(stats[:, 6 * n:6 * n + 6], rows[:, n * 512:(n + 1) * 512]), waits)
            aggregate, r = small_columns(2), small_columns()
            got = dve(lambda e: e.bn_aggr(aggregate, stats), [got])
            got = rsqrt_column(r, aggregate[:, 1:2], 1.0, eps_column, [got])
            return ts(rows if out is None else out, rows, aggregate[:, 0:1], r, ALU.subtract, ALU.mult, [got])

        def load_rows(label, pieces):
            sem = semaphore(f"{label}_loaded")
            held = []
            for n, source in enumerate(pieces):
                t, free = scratch.get(tick)
                token = load(t[:, 0:source.shape[1]], source.broadcast_to([P, source.shape[1]]), sem, 16 * (n + 1), free)
                held.append(t)
            return held, token

        def gain_and_shift(label, gain, shift, waits):
            for half in range(2):
                cols = slice(half * 512, (half + 1) * 512)
                (g, b), there = load_rows(f"{label}{half}", [dram[gain][:, cols], dram[shift][:, cols]])
                for t in range(TT):
                    got = tt(x_rows[t][:, cols], x_rows[t][:, cols], g[:, :], ALU.mult, [there, *waits])
                    x_ready[t] = tt(x_rows[t][:, cols], x_rows[t][:, cols], b[:, :], ALU.add, [got])
                scratch.put(g, [got])
                scratch.put(b, [x_ready[-1]])

        def gate_rows(v):
            held = []
            for half in range(2):
                bank, free = side_banks.get(tick)
                diagonal, diagonal_free = scratch.get(tick)
                for n in range(4):
                    k = 4 * half + n
                    built = ts(diagonal[:, n * P:(n + 1) * P], ident[:, :], mod[:, v, k:k + 1], None, ALU.mult, None,
                               [mod_ready[v], *diagonal_free])
                done = mm(bank[:, :], ones_all[:, :], diagonal[:, :], True, True, [built, *free], signal=True)
                got = copy(diagonal[:, :], bank[:, :], [done])
                side_banks.put(bank, [got])
                held.append((diagonal, got))
            return held

        def modulated_residual(v, label, x, waits, project_it):
            gates = gate_rows(v)

            def consume(t, cols, bank, done):
                gate, gate_ready = gates[cols.start // 512]
                product, free = scratch.get(tick)
                moved = tt(product[:, :], bank[:, :], gate[:, :], ALU.mult, [done, gate_ready, *free])
                x_ready[t] = stt(x_rows[t][:, cols], x_rows[t][:, cols], ALPHA, product[:, :], ALU.mult, ALU.add,
                                 [moved, x_ready[t]])
                scratch.put(product, [x_ready[t]])
                return moved

            project_it(label, x, waits, consume)
            for gate, _ in gates:
                scratch.put(gate, [x_ready[-1]])

        for t in range(TT):
            x_ready[t] = normalise_rows(x_rows[t], D, EPS5, [x_ready[t]])

        second = ExitStack()
        r_T, k_T, v_T = (place(second, name, [P, MIX // P, S]) for name in ("r_T", "k_T", "v_T"))
        lora_in = place(second, "lora_in", [P, S])
        gd_T = place(second, "gd_T", [P, 2, S])
        with ExitStack() as phase:
            h2_T = pair(phase, "h2_T", [P, KT, S])
            u_T = place(phase, "u_T", [P, MIX // P, S])
            v_sg = pair(phase, "v_sg", [P, MIX])
            w_s = place(phase, "w_s", [P, 4 * P])
            w_sp = pair(phase, "w_sp", [P, 4 * P])
            shifted = [place(phase, f"shifted{n}", [P, 1 + S]) for n in range(2)]
            h2_ready = turn_scaled(x_rows, [[x_ready[t]] for t in range(TT)], *h2_T, lambda k: fold[:, 0, k:k + 1], TT,
                                   folded, lambda k: fold[:, 1, k:k + 1])
            gain_and_shift("emb_ln", "emb_ln_g", "emb_ln_b", h2_ready)

            sem_ws = semaphore("w_s_loaded")
            loaded = load(w_s[:, :], dram["w_s"].rearrange("s g t -> s (g t)"), sem_ws, 16, fence)
            kept = pool(lambda e: e.affine_select(out=w_s[:, :], in_=w_s[:, :], pattern=[[0, 4], [1, P]],
                                                  compare_op=ALU.is_ge, fill=0.0, base=0, channel_multiplier=-1), [loaded])
            w_sp_ready = split(w_sp[0][:, :], w_sp[1][:, :], w_s[:, :], [kept])
            pads = [pool(lambda e, n=n: e.memset(shifted[n][:, 0:1], 0.0), []) for n in range(2)]

            u_ready = []
            for n in range(4):
                bank, done = feature_unit(f"pu.{n}", h2_T, waits=h2_ready)
                u_ready.append(act(u_T[:, n, :], bank[:, :], ACT.Gelu_apprx_tanh, [done]))
                unit_banks.put(bank, [u_ready[-1]])
            held = [side_banks.get(tick) for _ in range(TT)]
            pv_done = token_units("pv", h2_T, TT, [b for b, _ in held], [f for _, f in held])

            branch_tokens = []

            def spatial_gating():
                (g, b, b_s), there = load_rows("sg_ln", [dram["sg_ln_g"], dram["sg_ln_b"], dram["b_s"]])
                v_free = []
                for t, (bank, _) in enumerate(held):
                    v, free = scratch.get()
                    got = act(v[:, :], bank[:, :], ACT.Gelu_apprx_tanh, [pv_done[t], *free])
                    side_banks.put(bank, [got])
                    got = normalise_rows(v[:, :], MIX, EPS5, [got])
                    got = tt(v[:, :], v[:, :], g[:, :], ALU.mult, [got, there])
                    got = tt(v[:, :], v[:, :], b[:, :], ALU.add, [got])
                    both = split(v_sg[0][:, :], v_sg[1][:, :], v[:, :], [got, *v_free])
                    scratch.put(v, both)
                    yield
                    mixed, free = side_banks.get()
                    for n in range(4):
                        cols = slice(n * P, (n + 1) * P)
                        done = mm3(mixed[:, cols], (v_sg[0][:, cols], v_sg[1][:, cols]), (w_sp[0][:, cols], w_sp[1][:, cols]),
                                   True, True, [*both, *w_sp_ready, *free], signal=n == 3)
                    v_free = [done]
                    s, free = scratch.get()
                    tok = slice(t * P, (t + 1) * P)
                    got = tt(s[:, :], mixed[:, :], b_s[:, :], ALU.add, [done, *free])
                    side_banks.put(mixed, [got])
                    s4 = s[:, :].rearrange("p (g c) -> p g c", c=P)
                    got = tt(s4, s4, u_T[:, :, tok], ALU.mult, [got, u_ready[-1]])
                    both = split(branch[0][:, 0:4, tok], branch[1][:, 0:4, tok], s4, [got])
                    scratch.put(s, both)
                    branch_tokens.extend(both)
                    yield
                for t in (g, b, b_s):
                    scratch.put(t, both)

            spawn(spatial_gating())
            shifted_slots = Slots(shifted)
            rwkv_ready = []
            for n in range(15):
                bank, done = feature_unit(f"rwkv.{n}", h2_T)
                p, free = shifted_slots.get(tick)
                raw_copy = copy(p[:, 1:1 + S], bank[:, :], [done, *free])
                unit_banks.put(bank, [raw_copy])
                change, free = scratch.get(tick)
                got = tt(change[:, :], p[:, 0:S], p[:, 1:1 + S], ALU.subtract, [raw_copy, *pads, *free])
                if n < 12:
                    target = (r_T, k_T, v_T)[n // 4][:, n % 4, :]
                else:
                    target = lora_in[:, :] if n == 12 else gd_T[:, n - 13, :]
                got = stt(target, change[:, :], column("mu_shift_2", n), p[:, 1:1 + S], ALU.mult, ALU.add, [got])
                scratch.put(change, [got])
                shifted_slots.put(p, [got])
                rwkv_ready.append(got)
            finish_all()
            tanh_ready = act(lora_in[0:HALF, :], lora_in[0:HALF, :], ACT.Tanh, [rwkv_ready[12]])
            gd_ready = act(gd_T[:, :, :], gd_T[:, :, :], ACT.Sigmoid, [rwkv_ready[-1]])
        fence = q.latest()

        with ExitStack() as phase:
            FW = MIX // P
            lora_w = place(phase, "lora_w", [P, MIX])
            g_up = place(phase, "g_up", [P, 2, MIX])
            keep = place(phase, "keep", [P, S])
            mask = place(phase, "mask", [P, 4, P])
            levels = place(phase, "levels", [P, 6, P])
            AR = place(phase, "AR", [P, 2, S])
            Bw = place(phase, "Bw", [P, S])
            Kw = place(phase, "Kw", [P, S])
            bonus = place(phase, "bonus", [P, S])
            turned4 = [place(phase, f"tok_{n}", [P, TT, P]) for n in ("a", "b", "k", "v")]
            y0 = place(phase, "y0", [P, S])
            Q_T = place(phase, "Q_T", [P, S])
            P_T = place(phase, "P_T", [P, NC, P])
            Z = place(phase, "Z", [P, NC, P])
            LM = place(phase, "LM", [P, 4, 4, P])
            N, X, Y, W, BT = (place(phase, n, [P, 4, P]) for n in ("N_", "X_", "Y_", "W_", "BT_"))
            LkV = place(phase, "LkV", [P, 4, HALF])
            G = place(phase, "G_", [P, 2, P])
            H = place(phase, "H_", [P, 2, P])
            log2_shift = 20
            for _ in range(3):
                bank, free = unit_banks.get()
                side_banks.put(bank, free)
            for engine in ("act", "dve", "pe", "pool"):
                q.wait(engine, fence)
            sem_lora = semaphore("lora_loaded")
            load(lora_w[0:HALF, :], dram["w_up"], sem_lora, 16, fence)
            load(lora_w[HALF:P, :], dram["a_up"], sem_lora, 32)
            load(g_up[:, 0, :], dram["g_up"][0:P, :], sem_lora, 48)
            zeroed = pool(lambda e: e.memset(g_up[:, 1, :], 0.0), [])
            lora_ready = load(g_up[0:32, 1, :], dram["g_up"][P:160, :], sem_lora, 64, [zeroed])
            pool(lambda e: e.memset(keep[:, :], 1.0), [])
            pool(lambda e: e.memset(keep[:, :].rearrange("p (c t) -> p c t", t=CHUNK)[:, :, 0:1], 0.0), [])
            pool(lambda e: e.memset(mask[:, :, :], 1.0), [])
            pool(lambda e: e.memset(mask[0:CHUNK, :, CHUNK:P], 0.0), [])
            for n in range(4):
                pool(lambda e, n=n: e.affine_select(out=mask[:, n, :], in_=mask[:, n, :], pattern=[[1, P]],
                                                    compare_op=ALU.is_gt if n % 2 == 0 else ALU.is_ge, fill=0.0, base=0,
                                                    channel_multiplier=-1), [])
            pool(lambda e: e.memset(levels[:, :, :], 1.0), [])
            for n in range(5):
                size = 2 ** (n + 1)
                pat = [[size, P // size], [0, size]]
                pool(lambda e, n=n, pat=pat: e.affine_select(
                    out=levels[:, n, :], in_=levels[:, n, :], pattern=[[-a, b] for a, b in pat], compare_op=ALU.is_ge,
                    fill=0.0, base=0, channel_multiplier=1), [])
                pool(lambda e, n=n, pat=pat, size=size: e.affine_select(
                    out=levels[:, n, :], in_=levels[:, n, :], pattern=pat, compare_op=ALU.is_ge,
                    fill=0.0, base=size - 1, channel_multiplier=-1), [])
            tt(levels[:, 5, :], ones_head[:, :], levels[:, 4, :], ALU.subtract, [], engine="pool")
            for n in range(4, 0, -1):
                tt(levels[:, n, :], levels[:, n, :], levels[:, n - 1, :], ALU.subtract, [], engine="pool")
            masks_ready = tt(levels[:, 0, :], levels[:, 0, :], ident[:, :], ALU.subtract, [], engine="pool")
            pool(lambda e: e.memset(eps[:, 3:4], 0.5 * log2_shift * math.log(2.0)), [])
            masks_ready = pool(lambda e: e.memset(small[:, 0:1], 0.0), [])
            for engine in ("act", "dve", "pe"):
                q.wait(engine, [lora_ready, masks_ready, tanh_ready, gd_ready, rwkv_ready[-1]])

            def four(ap):
                return ap.rearrange("p (o c) -> p o c", o=1).broadcast_to([P, 4, P])

            f_free = []
            for f in range(FW):
                cols = slice(f * P, (f + 1) * P)
                bank, free = side_banks.get()
                done = mm(bank[:, :], lora_w[0:HALF, cols], lora_in[0:HALF, :], True, True, free, signal=True)
                log_w, free = scratch.get()
                got = act(log_w[:, :], bank[:, :], ACT.Sigmoid, [done, *free], bias=column("w0_2", f))
                side_banks.put(bank, [got])
                bank, free = side_banks.get()
                done = mm(bank[:, :], lora_w[HALF:P, cols], lora_in[HALF:P, :], True, True, free, signal=True)
                a, free = scratch.get()
                a_ready = act(a[:, :], bank[:, :], ACT.Sigmoid, [done, *free], bias=column("a0_2", f))
                side_banks.put(bank, [a_ready])
                scaled = ts(log_w[:, :], log_w[:, :], -math.exp(-0.5), None, ALU.mult, None, [got])
                total, free = scratch.get()
                summed = dve(lambda e, total=total, log_w=log_w: e.tensor_tensor_scan(
                    total[:, :], keep[:, :], log_w[:, :], 0.0, ALU.mult, ALU.add), [scaled, *free])
                before = tt(log_w[:, :], total[:, :], log_w[:, :], ALU.subtract, [summed])
                w_before = act(log_w[:, :], log_w[:, :], ACT.Exp, [before])
                w_all, free = scratch.get()
                w_ready = act(w_all[:, :], total[:, :], ACT.Exp, [summed, *free])
                got = tt(AR[:, 1, :], r_T[:, f, :], w_all[:, :], ALU.mult, [w_ready, *f_free])
                last_w = small_columns(NC)
                ends = w_all[:, :].rearrange("p (c t) -> p c t", t=CHUNK)[:, :, CHUNK - 1:CHUNK]
                last_w_ready = dve(lambda e, last_w=last_w, ends=ends: e.tensor_copy(
                    last_w.rearrange("p (c o) -> p c o", o=1), ends), [w_ready])
                scratch.put(w_all, [got, last_w_ready])
                sq, free = scratch.get()
                got = act(sq[:, :], k_T[:, f, :], ACT.Square, free, scale=column("k_k_2", f))
                stat, free = stat_bank.get()
                done = mm(stat[:, :], ones_head[:, :], sq[:, :], True, True, [got, *free], signal=True)
                clamped = ts(sq[:, :], stat[:, :], 1e-24, None, ALU.max, None, [done])
                stat_bank.put(stat, [clamped])
                got = act(sq[:, :], sq[:, :], ACT.Ln, [clamped], scale=2.0 ** log2_shift)
                got = act(sq[:, :], sq[:, :], ACT.Exp, [got], scale=-0.5, bias=eps[:, 3:4])
                kk, free = scratch.get()
                kk_ready = stt(kk[:, :], k_T[:, f, :], column("k_k_2", f), sq[:, :], ALU.mult, ALU.mult, [got, *free])
                scratch.put(sq, [kk_ready])
                a_done = stt(AR[:, 0, :], kk[:, :], -1.0, log_w[:, :], ALU.mult, ALU.mult, [kk_ready, w_before, *f_free])
                scratch.put(log_w, [a_done])
                b_ready = tt(kk[:, :], kk[:, :], a[:, :], ALU.mult, [a_done, a_ready])
                got = ts(a[:, :], a[:, :], column("k_a_2", f), one_minus_ka[:, f:f + 1], ALU.mult, ALU.add, [b_ready])
                k_ready = tt(a[:, :], a[:, :], k_T[:, f, :], ALU.mult, [got])
                prod, free = scratch.get()
                got = stt(prod[:, :], r_T[:, f, :], column("r_k_2", f), a[:, :], ALU.mult, ALU.mult, [k_ready, *free])
                stat, free = stat_bank.get()
                done = mm(stat[:, :], ones_head[:, :], prod[:, :], True, True, [got, *free], signal=True)
                bonus_ready = tt(bonus[:, :], stat[:, :], v_T[:, f, :], ALU.mult, [done, *f_free])
                stat_bank.put(stat, [bonus_ready])
                scratch.put(prod, [done])
                inverse, free = scratch.get()
                got = act(inverse[:, :], total[:, :], ACT.Exp, [summed, *free], scale=-1.0)
                tt(Bw[:, :], kk[:, :], inverse[:, :], ALU.mult, [got, b_ready, *f_free])
                bk_ready = tt(Kw[:, :], a[:, :], inverse[:, :], ALU.mult, [got, k_ready])
                scratch.put(inverse, [bk_ready])
                by_chunk = total[:, :].rearrange("p (c t) -> p c t", t=CHUNK)
                to_end, free = scratch.get()
                end_sum = small_columns(NC)
                got = dve(lambda e, o=end_sum, i=by_chunk: e.tensor_copy(
                    o.rearrange("p (c o) -> p c o", o=1), i[:, :, CHUNK - 1:CHUNK]), [summed])
                got = tt(to_end[:, :].rearrange("p (c t) -> p c t", t=CHUNK),
                         end_sum.rearrange("p (c o) -> p c o", o=1).broadcast_to([P, NC, CHUNK]), by_chunk,
                         ALU.subtract, [got, *free])
                scratch.put(total, [got])
                got = act(to_end[:, :], to_end[:, :], ACT.Exp, [got])
                be_ready = tt(kk[:, :], kk[:, :], to_end[:, :], ALU.mult, [got, bk_ready])
                ke_ready = tt(a[:, :], a[:, :], to_end[:, :], ALU.mult, [got, bk_ready])
                scratch.put(to_end, [ke_ready])
                sources = ((AR[:, 0, :], a_done), (kk[:, :], be_ready), (a[:, :], ke_ready), (v_T[:, f, :], None))
                turned_ready = []
                for n, (source, ready) in enumerate(sources):
                    bank, free = side_banks.get()
                    for i in range(TT):
                        done = transpose(bank[:, i * P:(i + 1) * P], source[:, i * P:(i + 1) * P], [ready, *free],
                                         signal=i == TT - 1)
                    got = copy(turned4[n][:, :, :], bank[:, :].rearrange("p (i c) -> p i c", c=P), [done, *f_free])
                    side_banks.put(bank, [got])
                    turned_ready.append(got)
                scratch.put(kk, turned_ready)
                scratch.put(a, turned_ready)
                A_tok, B_tok, K_tok, V_tok = turned4

                for half in range(2):
                    tiles = [2 * half, 2 * half + 1]
                    for m in range(4):
                        i, rows = tiles[m // 2], slice((m % 2) * HALF, (m % 2 + 1) * HALF)
                        tok = slice(i * P, (i + 1) * P)
                        bank, free = side_banks.get()
                        mm(bank[:, 0:2 * P], Bw[rows, tok], AR[rows, :, tok], True, True, [bk_ready, a_done, *free])
                        done = mm(bank[:, 2 * P:4 * P], Kw[rows, tok], AR[rows, :, tok], True, True, signal=True)
                        masked = tt(LM[:, m, :, :], bank[:, :].rearrange("p (n c) -> p n c", c=P), mask[:, :, :],
                                    ALU.mult, [done, *f_free])
                        side_banks.put(bank, [masked])
                    bank, free = side_banks.get()
                    for m in range(4):
                        done = transpose(bank[:, m * P:(m + 1) * P], LM[:, m, 0, :], [masked, *free], signal=m == 3)
                    got = copy(N[:, :, :], bank[:, :].rearrange("p (n c) -> p n c", c=P), [done, *f_free])
                    side_banks.put(bank, [got])
                    NT = LM[:, :, 0, :]
                    got = tt(X[:, :, :], N[:, :, :], four(levels[:, 0, :]), ALU.mult, [got, *f_free])
                    x_done = tt(X[:, :, :], X[:, :, :], four(ident[:, :]), ALU.add, [got])
                    got = tt(Y[:, :, :], NT, four(levels[:, 0, :]), ALU.mult, [masked, *f_free])
                    y_done = tt(Y[:, :, :], Y[:, :, :], four(ident[:, :]), ALU.add, [got])
                    bt_free = f_free
                    for level in range(1, 6):
                        got = tt(BT[:, :, :], NT, four(levels[:, level, :]), ALU.mult, [masked, *bt_free])
                        bank, free = side_banks.get()
                        for m in range(4):
                            done = mm(bank[:, m * P:(m + 1) * P], BT[:, m, :], X[:, m, :], True, True,
                                      [got, x_done, *free], signal=m == 3)
                        bt_free = [done]
                        w_done = copy(W[:, :, :], bank[:, :].rearrange("p (n c) -> p n c", c=P), [done, y_done])
                        side_banks.put(bank, [w_done])
                        bank_y, free = side_banks.get()
                        for m in range(4):
                            done = mm(bank_y[:, m * P:(m + 1) * P], W[:, m, :], Y[:, m, :], True, True,
                                      [w_done, y_done, *free], signal=m == 3)
                        if level < 5:
                            bank_x, free = side_banks.get()
                            for m in range(4):
                                done = mm(bank_x[:, m * P:(m + 1) * P], Y[:, m, :], W[:, m, :], True, True,
                                          free, signal=m == 3)
                            x_done = tt(X[:, :, :], X[:, :, :], bank_x[:, :].rearrange("p (n c) -> p n c", c=P), ALU.add,
                                        [done])
                            side_banks.put(bank_x, [x_done])
                        y_done = tt(Y[:, :, :], Y[:, :, :], bank_y[:, :].rearrange("p (n c) -> p n c", c=P), ALU.add,
                                    [done])
                        side_banks.put(bank_y, [y_done])
                    def head(m):
                        return slice((m % 2) * HALF, (m % 2 + 1) * HALF)
                    bank, free = side_banks.get()
                    for m in range(4):
                        done = mm(bank[:, m * HALF:(m + 1) * HALF], LM[:, m, 2, :], V_tok[:, tiles[m // 2], head(m)], True,
                                  True, [*turned_ready, masked, *free], signal=m == 3)
                    lkv_ready = copy(LkV[:, :, :], bank[:, 0:4 * HALF].rearrange("p (n c) -> p n c", c=HALF), [done, *f_free])
                    side_banks.put(bank, [lkv_ready])
                    bank, free = side_banks.get()
                    for m in range(4):
                        mm(bank[:, m * HALF:(m + 1) * HALF], Y[:, m, :], A_tok[:, tiles[m // 2], head(m)], True, True,
                           [y_done, *turned_ready, *free])
                        done = mm(bank[:, (4 + m) * HALF:(5 + m) * HALF], Y[:, m, :], LkV[:, m, :], True, True,
                                  [lkv_ready], signal=m == 3)
                    g_ready = copy(G[:, :, :], bank[:, 0:2 * P].rearrange("p (n c) -> p n c", c=P), [done, *f_free])
                    gh_ready = copy(H[:, :, :], bank[:, 2 * P:4 * P].rearrange("p (n c) -> p n c", c=P), [done])
                    side_banks.put(bank, [gh_ready])
                    bank_q, free_q = side_banks.get()
                    bank_y, free_y = side_banks.get()
                    for m in range(4):
                        rows, at = head(m), slice((m // 2) * P, (m // 2 + 1) * P)
                        mm(bank_q[rows, at], G[:, m // 2, rows], LM[:, m, 1, :], True, True, [gh_ready, *free_q])
                        mm(bank_y[rows, at], H[:, m // 2, rows], LM[:, m, 1, :], True, False, free_y)
                        done = mm(bank_y[rows, at], V_tok[:, tiles[m // 2], rows], LM[:, m, 3, :], False, True,
                                  signal=m == 3)
                    tok2 = slice(2 * half * P, 2 * (half + 1) * P)
                    q_ready = tt(Q_T[:, tok2], bank_q[:, 0:2 * P], AR[:, 1, tok2], ALU.add, [done, *f_free])
                    side_banks.put(bank_q, [q_ready])
                    y0_ready = copy(y0[:, tok2], bank_y[:, 0:2 * P], [done, *f_free])
                    side_banks.put(bank_y, [y0_ready])
                    for part in range(2):
                        rows = slice(part * CHUNK, (part + 1) * CHUNK)
                        bank, free = side_banks.get()
                        for n in range(2):
                            i = tiles[n]
                            mm(bank[:, n * P:(n + 1) * P], G[rows, n, :], B_tok[rows, i, :], True, True, free)
                            mm(bank[:, (2 + n) * P:(3 + n) * P], B_tok[rows, i, :], H[rows, n, :], True, False)
                            done = mm(bank[:, (2 + n) * P:(3 + n) * P], K_tok[rows, i, :], V_tok[rows, i, :], False, True,
                                      signal=n == 1)
                        for n in range(2):
                            c = 2 * tiles[n] + part
                            got = tt(P_T[:, c, :], bank[:, n * P:(n + 1) * P], ones_head[:, :], ALU.mult, [done, *f_free])
                            stt(P_T[:, c, :], ident[:, :], last_w[:, c:c + 1], P_T[:, c, :], ALU.mult, ALU.add,
                                [got, last_w_ready])
                            z_ready = tt(Z[:, c, :], bank[:, (2 + n) * P:(3 + n) * P], ones_head[:, :], ALU.mult, [done])
                        side_banks.put(bank, [z_ready])
                bank, free = side_banks.get()
                state = z_ready
                for c in range(1, NC - 1):
                    step_bank, step_free = side_banks.get()
                    done = mm(step_bank[:, 0:P], P_T[:, c, :], Z[:, c - 1, :], True, True, [state, *step_free], signal=True)
                    state = tt(Z[:, c, :], Z[:, c, :], step_bank[:, 0:P], ALU.add, [done])
                    side_banks.put(step_bank, [state])
                for c in range(1, NC):
                    tok = slice(c * CHUNK, (c + 1) * CHUNK)
                    done = mm(bank[:, tok], Z[:, c - 1, :], Q_T[:, tok], True, True, [state, q_ready, *free],
                              signal=c == NC - 1)
                later = slice(CHUNK, S)
                got = tt(y0[:, later], y0[:, later], bank[:, later], ALU.add, [done, y0_ready])
                side_banks.put(bank, [got])
                stat, free = stat_bank.get()
                done = mm(stat[:, :], ones_head[:, :], y0[:, :], True, True, [got, *free], signal=True)
                centred = stt(y0[:, :], stat[:, :], -1.0 / HALF, y0[:, :], ALU.mult, ALU.add, [done])
                stat_bank.put(stat, [centred])
                sq, free = scratch.get()
                got = act(sq[:, :], y0[:, :], ACT.Square, [centred, *free])
                stat, free = stat_bank.get()
                done = mm(stat[:, :], ones_head[:, :], sq[:, :], True, True, [got, *free], signal=True)
                scratch.put(sq, [done])
                r, got_ln, got = rsqrt_rows(stat[:, :], [done], HALF, EPSG)
                stat_bank.put(stat, [got_ln])
                got = tt(r[:, :], r[:, :], y0[:, :], ALU.mult, [got])
                got = ts(r[:, :], r[:, :], column("lnx_g_2", f), column("lnx_b_2", f), ALU.mult, ALU.add, [got])
                got = tt(r[:, :], r[:, :], bonus[:, :], ALU.add, [got])
                bank, free = side_banks.get()
                for n in range(2):
                    done = mm(bank[:, :], g_up[:, n, cols], gd_T[:, n, :], n == 0, n == 1, free, signal=n == 1)
                got = tt(r[:, :], r[:, :], bank[:, :], ALU.mult, [got, done])
                side_banks.put(bank, [got])
                both = split(branch[0][:, 4 + f, :], branch[1][:, 4 + f, :], r[:, :], [got])
                scratch.put(r, both)
                branch_tokens.extend(both)
                f_free = q.latest()
            for _ in range(3):
                unit_banks.put(*side_banks.get())
        second.close()
        fence = q.latest()

        modulated_residual(2, "w_out_2", branch, branch_tokens, token_projection)

        for t in range(TT):
            x_ready[t] = normalise_rows(x_rows[t], D, EPS5, [x_ready[t]])
        with ExitStack() as phase:
            h3_T = pair(phase, "h3_T", [P, KT, S])
            f_more = pair(phase, "f_more", [P, FT - KT, S])
            for engine in ("act", "dve", "pe", "pool"):
                q.wait(engine, fence)
            h3_ready = turn_scaled(x_rows, [[x_ready[t]] for t in range(TT)], *h3_T, lambda k: fold[:, 2, k:k + 1], TT,
                                   folded, lambda k: fold[:, 3, k:k + 1])
            gain_and_shift("ln1", "ln1_g", "ln1_b", h3_ready)

            def hidden(n):
                where, at = (branch, n) if n < KT else (f_more, n - KT)
                return where[0][:, at, :], where[1][:, at, :]

            f_ready = []
            for n in range(FT):
                bank, done = feature_unit(f"ffn_g.{n}", h3_T, waits=h3_ready)
                gate, free = scratch.get(tick)
                gated = act(gate[:, :], bank[:, :], ACT.Silu, [done, *free])
                unit_banks.put(bank, [gated])
                bank, done = feature_unit(f"ffn_u.{n}", h3_T)
                got = tt(gate[:, :], bank[:, :], gate[:, :], ALU.mult, [done, gated])
                unit_banks.put(bank, [got])
                both = split(*hidden(n), gate[:, :], [got, *fence])
                scratch.put(gate, both)
                f_ready.append(both)

            gates = gate_rows(5)
            held = [unit_banks.get(tick) for _ in range(3)] + [stat_bank.get(tick)] + [side_banks.get(tick) for _ in range(4)]
            for n in range(FT):
                u, (hi, lo), ready = take(f"ffn_out.{n}")
                f_hi, f_lo = hidden(n)
                for t in range(TT):
                    tok = slice(t * P, (t + 1) * P)
                    for half in range(2):
                        bank, free = held[2 * t + half]
                        cols = slice(half * 512, (half + 1) * 512)
                        last = n == FT - 1
                        done = mm3(bank[:, :], (f_hi[:, tok], f_lo[:, tok]), (hi[:, cols], lo[:, cols]), n == 0, last,
                                   [*ready, *f_ready[n], *free], signal=last or (t == TT - 1 and half == 1))
                        if last:
                            gate, gate_ready = gates[half]
                            product, free = scratch.get()
                            got = tt(product[:, :], bank[:, :], gate[:, :], ALU.mult, [done, gate_ready, *free])
                            x_ready[t] = stt(x_rows[t][:, cols], x_rows[t][:, cols], ALPHA, product[:, :], ALU.mult,
                                             ALU.add, [got, x_ready[t]])
                            scratch.put(product, [x_ready[t]])
                give_back(u, done)
            for gate, _ in gates:
                scratch.put(gate, [x_ready[-1]])
        for t in range(TT):
            x_ready[t] = normalise_rows(x_rows[t], D, EPS5, [x_ready[t]])
        gain_and_shift("ln2", "ln2_g", "ln2_b", [x_ready[-1]])
        sem_out = semaphore("out_stored")
        for t in range(TT):
            stored = load(out[t * P:(t + 1) * P, :], x_rows[t], sem_out, 16 * (t + 1), [x_ready[t]])
        q.wait("sync", [stored])

        block = whole.enter_context(nc.Block())

        @block.sync
        def _(eng):
            for step in q.steps["sync"]:
                step(eng)

        @block.scalar
        def _(eng):
            for step in q.steps["act"]:
                step(eng)

        @block.vector
        def _(eng):
            for step in q.steps["dve"]:
                step(eng)

        @block.gpsimd
        def _(eng):
            for step in q.steps["pool"]:
                step(eng)

        @block.tensor
        def _(eng):
            for step in q.steps["pe"]:
                step(eng)


def pack_weights(inputs):
    plan = unit_plan()
    packed = np.zeros((len(plan), P, UNIT), np.float32)
    for n, (_, array, kind, row, col) in enumerate(plan):
        w = np.asarray(inputs[array])[0]
        if kind == "F":
            part = w[:, col:col + P].reshape(KT, P, -1).transpose(1, 0, 2)
            packed[n].reshape(P, KT, P)[:, :, 0:part.shape[2]] = part
        elif kind == "T":
            packed[n] = w[row:row + 256, col:col + 512].reshape(2, P, 512).transpose(1, 0, 2).reshape(P, UNIT)
        else:
            packed[n] = w[row:row + P, :]
    return packed


def pack_columns(inputs):
    packed = np.zeros((N_COLUMNS, P), np.float32)
    for name, size in COLUMN_VECTORS:
        v = np.asarray(inputs[name]).reshape(-1)
        if size == HALF:
            v = np.concatenate([v, v])
        at = COLUMN_AT[name]
        packed.reshape(-1)[at * P:at * P + v.size] = v
    return np.ascontiguousarray(packed.T)


def kernel(**inputs):
    import concourse.bacc as bacc
    from concourse.bass_utils import run_bass_kernel_spmd

    arrays = {"weights": pack_weights(inputs), "columns": pack_columns(inputs)}

    def plain(name, source, shape):
        arrays[name] = np.ascontiguousarray(np.asarray(inputs[source]).reshape(shape))

    plain("x", "x", (S, D))
    plain("mem", "mem", (M, D))
    plain("w_ada", "w_ada_2", (D, 6 * D))
    for name in ("lambda_q1", "lambda_k1", "lambda_q2", "lambda_k2"):
        plain(name, name, (1, HALF))
    for name, size in (("emb_ln_g", D), ("emb_ln_b", D), ("ln1_g", D), ("ln1_b", D), ("ln2_g", D), ("ln2_b", D),
                       ("sg_ln_g", MIX), ("sg_ln_b", MIX), ("b_s", MIX)):
        plain(name, name + "_2", (1, size))
    plain("w_up", "w_up_2", (64, MIX))
    plain("a_up", "a_up_2", (64, MIX))
    plain("g_up", "g_up_2", (160, MIX))
    arrays["w_s"] = np.ascontiguousarray(np.asarray(inputs["w_s_2"])[0].transpose(2, 0, 1))
    nc = bacc.Bacc("TRN2", target_bir_lowering=False, num_devices=1)
    dram = {}
    for name, a in arrays.items():
        dram[name] = nc.dram_tensor("in_" + name, a.shape, FP32, kind="ExternalInput").ap()
    out = nc.dram_tensor("out", (S, D), FP32, kind="ExternalOutput").ap()
    build(nc, dram, out)
    result = run_bass_kernel_spmd(nc, [{"in_" + n: a for n, a in arrays.items()}], core_ids=[0])
    return result.results[0]["out"].reshape(1, S, D)
```

```python
import math
from contextlib import ExitStack

import numpy as np

import concourse.bass as bass
from concourse import mybir

FP32 = mybir.dt.float32
FP32R = mybir.dt.float32r
ACT = mybir.ActivationFunctionType
ALU = mybir.AluOpType
AX = mybir.AxisListType.X

P = 128
D = 1024
S = 512
M = 256
KT = D // P
TT = S // P
CONV_K = 31
HEADS = 8
HALF = 64
X_HEADS = 4
X_DIM = D // X_HEADS
LAMBDA_INIT = 0.8 - 0.6 * math.exp(-0.3 * 0)
MIX = D // 2
FFN = ((8 * D + 3 * 256 - 1) // (3 * 256)) * 256
FT = FFN // P
ALPHA = 2 ** 0.25
CHUNK = 64
NC = S // CHUNK
UNIT = 1024
MASKED = -1e30
LN_EXP = "natural_log_exp_and_others"
MERGE_LEAD = 3

COLUMN_VECTORS = [
    ("norm_g", D), ("mem_norm_g", D), ("conv_dw_b", D), ("conv_ln_g", D), ("conv_ln_b", D),
    ("diff_qn_g", HALF), ("diff_kn_g", HALF), ("diff_subln_g", P), ("x_qn_g", X_DIM), ("x_kn_g", X_DIM),
    ("emb_ln_g_2", D), ("emb_ln_b_2", D), ("mu_shift_2", 1824), ("w0_2", MIX), ("a0_2", MIX),
    ("k_k_2", MIX), ("k_a_2", MIX), ("r_k_2", MIX), ("lnx_g_2", MIX), ("lnx_b_2", MIX),
    ("ln1_g_2", D), ("ln1_b_2", D), ("b_ada_2", 6 * D), ("c_2", D), ("conv_dw", CONV_K * D),
]
COLUMN_AT = {}
_n = 0
for _name, _size in COLUMN_VECTORS:
    COLUMN_AT[_name] = _n
    _n += -(-_size // P)
N_COLUMNS = _n

W_IN_AT = {"conv_a": 0, "conv_b": 1024, "conv_gate": 2048, "dq": 3072, "dk": 4096, "dv": 5120,
           "d_gate": 6144, "xq": 7168, "x_gate": 8192, "merge": 9216}


GATE_OF = {0: 0, 1: 2, 2: 1}


def unit_plan():
    plan = []

    def f(label, array, column):
        plan.append((label, array, "F", 0, column))

    def t(label, array, column):
        for pair in range(KT // 2):
            plan.append((f"{label}.{pair}", array, "T", 256 * pair, column))

    def project(branch, w):
        for d in range(KT + MERGE_LEAD):
            if d < KT:
                f(f"merge{branch}.{d}", "w_in", W_IN_AT["merge"] + GATE_OF[branch] * D + d * P)
            if d >= MERGE_LEAD:
                f(f"proj{branch}.{d - MERGE_LEAD}", w, (d - MERGE_LEAD) * P)

    for n in range(KT):
        f(f"conv_b.{n}", "w_in", W_IN_AT["conv_b"] + n * P)
        f(f"conv_a.{n}", "w_in", W_IN_AT["conv_a"] + n * P)
        f(f"conv_gate.{n}", "w_in", W_IN_AT["conv_gate"] + n * P)
    project(0, "w_conv_proj")
    for n in range(KT):
        f(f"xk.{n}", "w_mem_kv", n * P)
    for half in range(2):
        t(f"xv{half}", "w_mem_kv", D + half * 512)
    for h in range(X_HEADS):
        for c in range(2):
            f(f"xq.{2 * h + c}", "w_in", W_IN_AT["xq"] + (2 * h + c) * P)
        for c in range(2):
            f(f"x_gate.{2 * h + c}", "w_in", W_IN_AT["x_gate"] + (2 * h + c) * P)
    project(1, "w_x_proj")
    for h in range(HEADS):
        f(f"dq.{h}", "w_in", W_IN_AT["dq"] + h * P)
        f(f"dk.{h}", "w_in", W_IN_AT["dk"] + h * P)
        if h % 4 == 0:
            t(f"dv{h // 4}", "w_in", W_IN_AT["dv"] + (h // 4) * 512)
        f(f"d_gate.{h}", "w_in", W_IN_AT["d_gate"] + h * P)
    project(2, "w_diff_proj")
    for half in range(2):
        t(f"w_out{half}", "w_out", half * 512)
    for n in range(4):
        f(f"pu.{n}", "w_in_2", n * P)
    t("pv", "w_in_2", MIX)
    for n in range(14):
        f(f"rwkv.{n}", "w_in_2", 2 * MIX + n * P)
    f("rwkv.14", "w_in_2", 2 * MIX + 14 * P)
    for half in range(2):
        t(f"w_out_2{half}", "w_out_2", half * 512)
    for n in range(FT):
        f(f"ffn_g.{n}", "w_ffn_in_2", n * P)
        f(f"ffn_u.{n}", "w_ffn_in_2", FFN + n * P)
    for n in range(FT):
        plan.append((f"ffn_out.{n}", "w_ffn_out_2", "O", n * P, 0))
    return plan




class Slots:

    def __init__(self, tensors):
        self.ready = [(t, []) for t in tensors]

    def get(self, tick=None):
        while not self.ready:
            assert tick is not None, "no slot is free"
            tick()
        return self.ready.pop(0)

    def put(self, tensor, last_readers):
        self.ready.append((tensor, list(last_readers)))


class Queues:

    def __init__(self, progress):
        self.progress = progress
        self.steps = {e: [] for e in progress}
        self.count = {e: 0 for e in progress}
        self.reached = {e: {} for e in progress}

    def wait(self, engine, tokens):
        for token in tokens:
            if token is None:
                continue
            sem, value = token
            if self.reached[engine].get(sem, 0) < value:
                self.reached[engine][sem] = value
                self.steps[engine].append(lambda eng, sem=sem, value=value: eng.wait_ge(sem, value))

    def add(self, engine, make, waits, count=True):
        if engine == "pool" and self.count[engine]:
            waits = [*waits, (self.progress[engine], self.count[engine])]
        self.wait(engine, waits)
        if not count:
            self.steps[engine].append(make)
            return None
        sem = self.progress[engine]
        self.count[engine] += 1
        self.steps[engine].append(lambda eng: make(eng).then_inc(sem, 1))
        return (sem, self.count[engine])

    def latest(self):
        return [(self.progress[e], self.count[e]) for e in self.progress if self.count[e]]


def build(nc, dram, out):
    with ExitStack() as whole:
        def semaphore(name):
            return whole.enter_context(nc.semaphore(name))

        q = Queues({e: semaphore(f"{e}_progress") for e in ("pe", "act", "dve", "pool")})
        q.steps["sync"], q.reached["sync"] = [], {}

        def place(stack, name, shape, dtype=FP32):
            return stack.enter_context(nc.sbuf_tensor(name, shape, dtype))

        def pair(stack, name, shape):
            return (place(stack, name + "_hi", shape, FP32R), place(stack, name + "_lo", shape, FP32R))

        table = [None]

        def act(o, i, func, waits, bias=0.0, scale=1.0, accum=None):
            if func in (ACT.Exp, ACT.Ln) and table[0] != LN_EXP:
                q.steps["act"].append(lambda e: e.preload_act_table_set(LN_EXP))
                table[0] = LN_EXP
            elif func not in (ACT.Exp, ACT.Ln, ACT.Copy, ACT.Square):
                table[0] = func
            if accum is None:
                return q.add("act", lambda e: e.activation(o, i, func, bias=bias, scale=scale), waits)
            return q.add("act", lambda e: e.activation(o, i, func, bias=bias, scale=scale, accum_out=accum), waits)

        def copy(o, i, waits):
            return act(o, i, ACT.Copy, waits)

        def tt(o, a, b, op, waits, engine="dve"):
            return q.add(engine, lambda e: e.tensor_tensor(o, a, b, op), waits)

        def ts(o, a, s1, s2, op0, op1, waits, engine="dve"):
            if op1 is None:
                return q.add(engine, lambda e: e.tensor_scalar(o, a, s1, None, op0), waits)
            return q.add(engine, lambda e: e.tensor_scalar(o, a, s1, s2, op0, op1), waits)

        def stt(o, a, s, b, op0, op1, waits):
            return q.add("dve", lambda e: e.scalar_tensor_tensor(out=o, in0=a, scalar=s, in1=b, op0=op0, op1=op1), waits)

        def dve(make, waits):
            return q.add("dve", make, waits)

        def pool(make, waits):
            return q.add("pool", make, waits)

        def mm(o, lhsT, rhs, start, stop, waits=(), signal=False):
            return q.add("pe", lambda e: e.matmul(o, lhsT, rhs, start=start, stop=stop), waits, count=signal)

        def transpose(o, i, waits, signal=False):
            ident_ap = ident[0:i.shape[0], 0:i.shape[0]]
            return q.add("pe", lambda e: e.transpose(o, i, ident_ap), waits, count=signal)

        def mm3(o, lhs, rhs, start, stop, waits=(), signal=False):
            mm(o, lhs[0], rhs[0], start, False, waits)
            mm(o, lhs[0], rhs[1], False, False)
            return mm(o, lhs[1], rhs[0], False, stop, (), signal)

        def load(o, i, sem, total, waits=()):
            q.wait("sync", waits)
            q.steps["sync"].append(lambda e: e.dma_start(o, i).then_inc(sem, 16))
            return (sem, total)

        def view(t):
            return t.bitcast(FP32)

        def split(hi, lo, value, waits):
            got_hi = copy(hi, value, waits)
            got_lo = tt(lo, value, view(hi), ALU.subtract, [*waits, got_hi])
            return [got_hi, got_lo]

        banks = [whole.enter_context(nc.psum_tensor(f"bank{n}", [P, 512], FP32)) for n in range(8)]
        unit_banks = Slots(banks[0:3])
        stat_bank = Slots(banks[3:4])
        side_banks = Slots(banks[4:8])

        RAW, SPLIT = 4, 3
        raw = [place(whole, f"raw{n}", [P, UNIT]) for n in range(RAW)]
        parts = [pair(whole, f"weight{n}", [P, UNIT]) for n in range(SPLIT)]
        ident = place(whole, "ident", [P, P])
        ones_all = place(whole, "ones_all", [P, P])
        ones_head = place(whole, "ones_head", [P, P])
        columns = place(whole, "columns", [P, N_COLUMNS])
        scratch = Slots([place(whole, f"scratch{n}", [P, S]) for n in range(7)])
        eps = place(whole, "eps", [P, 4])
        small = place(whole, "small", [P, 256])
        mod = place(whole, "mod", [P, 6, KT])

        def column(name, n=0):
            at = COLUMN_AT[name] + n
            return columns[:, at:at + 1]

        small_at = [0]

        def small_columns(n=1):
            at = small_at[0]
            if at + n > 256:
                at = 0
            small_at[0] = at + n
            return small[:, at:at + n]

        sem_columns = semaphore("columns_loaded")
        columns_ready = load(columns[:, :], dram["columns"], sem_columns, 16)
        pool(lambda e: e.memset(ident[:, :], 0.0), [])
        pool(lambda e: e.memset(ones_all[:, :], 1.0), [])
        zeroed = pool(lambda e: e.memset(ones_head[:, :], 0.0), [])
        pool(lambda e: e.memset(eps[:, 0:1], 1e-6), [])
        pool(lambda e: e.memset(eps[:, 1:2], 1e-5), [])
        pool(lambda e: e.memset(eps[:, 2:3], 64e-5), [])
        pool(lambda e: e.memset(eps[:, 3:4], 0.0), [])
        pool(lambda e: e.memset(ones_head[0:HALF, 0:HALF], 1.0), [zeroed])
        cleared = pool(lambda e: e.memset(ones_head[HALF:P, HALF:P], 1.0), [])
        consts_ready = pool(lambda e: e.affine_select(
            out=ident[:, :], in_=ident[:, :], pattern=[[-1, P]], compare_op=ALU.not_equal, fill=1.0,
            base=0, channel_multiplier=1), [cleared])
        for engine in ("pe", "act", "dve"):
            q.wait(engine, [consts_ready, columns_ready])
        q.wait("pool", [columns_ready, consts_ready])
        EPS6, EPS5, EPSG = eps[:, 0:1], eps[:, 1:2], eps[:, 2:3]

        tasks = []

        def spawn(generator):
            tasks.append(generator)
            return generator

        def advance(task):
            try:
                next(task)
            except StopIteration:
                tasks.remove(task)

        def tick():
            for task in list(tasks):
                if task in tasks:
                    advance(task)

        def slot(slots):
            while not slots.ready:
                yield
            return slots.get()

        def finish(task):
            for _ in range(2000):
                if task not in tasks:
                    return
                tick()
            raise AssertionError("a side task waits for ever")

        def finish_all():
            idle = 0
            while tasks:
                before = sum(q.count.values())
                tick()
                idle = idle + 1 if sum(q.count.values()) == before else 0
                assert idle < 1000, "the side tasks wait for each other"

        plan = unit_plan()
        raw_sems = [semaphore(f"raw{n}_loaded") for n in range(RAW)]
        raw_free = [[] for _ in range(RAW)]
        part_free = [[] for _ in range(SPLIT)]
        part_ready = {}
        raw_ready = {}
        taken = [0]

        def load_unit(u):
            if u < len(plan):
                n = u % RAW
                raw_ready[u] = load(raw[n][:, :], dram["weights"][u], raw_sems[n], 16 * (u // RAW + 1), raw_free[n])

        def split_unit(u):
            if u < len(plan):
                n, hi, lo = u % RAW, *parts[u % SPLIT]
                part_ready[u] = split(hi[:, :], lo[:, :], raw[n][:, :], [raw_ready[u], *part_free[u % SPLIT]])
                raw_free[n] = part_ready[u]
                load_unit(u + RAW)

        for u in range(RAW):
            load_unit(u)

        def start_weights():
            for u in range(SPLIT):
                split_unit(u)

        def take(label):
            u = taken[0]
            assert plan[u][0] == label, (plan[u][0], label)
            taken[0] += 1
            return u, parts[u % SPLIT], part_ready[u]

        def give_back(u, last_product):
            part_free[u % SPLIT] = [last_product]
            split_unit(u + SPLIT)

        def feature_unit(label, x, width=S, waits=()):
            u, (hi, lo), ready = take(label)
            bank, free = unit_banks.get(tick)
            for k in range(KT):
                cols = slice(k * P, (k + 1) * P)
                done = mm3(bank[:, 0:width], (hi[:, cols], lo[:, cols]), (x[0][:, k, 0:width], x[1][:, k, 0:width]),
                           k == 0, k == KT - 1, [*ready, *free, *waits] if k == 0 else (), signal=k == KT - 1)
                if k == KT // 2 - 1:
                    tick()
            give_back(u, done)
            tick()
            return bank, done

        def token_units(label, x, tiles, out_banks, frees, waits=()):
            done = None
            for n in range(KT // 2):
                u, (hi, lo), ready = take(f"{label}.{n}")
                for t in range(tiles):
                    tok = slice(t * P, (t + 1) * P)
                    for j in range(2):
                        k = 2 * n + j
                        cols = slice(j * 512, (j + 1) * 512)
                        last = n == KT // 2 - 1 and j == 1
                        done = mm3(out_banks[t][:, :], (x[0][:, k, tok], x[1][:, k, tok]), (hi[:, cols], lo[:, cols]),
                                   k == 0, last, [*ready, *frees[t], *waits] if j == 0 else (),
                                   signal=last or (t == tiles - 1 and j == 1))
                        if last:
                            tile_done[t] = done
                    if t == tiles // 2 - 1:
                        tick()
                give_back(u, done)
                tick()
            return list(tile_done[:tiles])

        tile_done = [None] * TT

        def rsqrt_rows(source, waits, n, bias, width=S):
            r, free = scratch.get()
            got_ln = act(r[:, 0:width], source, ACT.Ln, [*waits, *free], bias=bias, scale=1.0 / n)
            got = act(r[:, 0:width], r[:, 0:width], ACT.Exp, [got_ln], scale=-0.5)
            return r, got_ln, got

        def rsqrt_column(o, i, scale, bias, waits):
            t = small_columns()
            got_ln = act(t, i, ACT.Ln, waits, bias=bias, scale=scale)
            return act(o, t, ACT.Exp, [got_ln], scale=-0.5)

        def turn_scaled(source, ready, hi, lo, gains, tiles, free, shifts=None):
            tokens = []
            for k in range(KT):
                bank, bank_free = side_banks.get()
                width = tiles * P
                for t in range(tiles):
                    turned = transpose(bank[:, t * P:(t + 1) * P], source[t][:, k * P:(k + 1) * P],
                                       [*ready[t], *bank_free], signal=t == tiles - 1)
                full, scratch_free = scratch.get()
                if shifts is None:
                    got = ts(full[:, 0:width], bank[:, 0:width], gains(k), None, ALU.mult, None, [turned, *scratch_free])
                else:
                    got = ts(full[:, 0:width], bank[:, 0:width], gains(k), shifts(k), ALU.mult, ALU.add,
                             [turned, *scratch_free])
                side_banks.put(bank, [got])
                both = split(hi[:, k, 0:width], lo[:, k, 0:width], full[:, 0:width], [got, *free])
                scratch.put(full, both)
                tokens += both
            return tokens[-2:]

        y_T = place(whole, "y_T", [P, KT, S])
        x_rows = [y_T[:, 2 * t:2 * t + 2, :].rearrange("p a b -> p (a b)") for t in range(TT)]
        first = ExitStack()
        branch = pair(first, "branch", [P, KT, S])
        h_T = pair(first, "h_T", [P, KT, S])

        ada = [place(first, f"ada{n}", [P, D]) for n in range(2)]
        ada_sum = place(first, "ada_sum", [P, D])
        silu_c = place(first, "silu_c", [P, KT])
        ada_sems = [semaphore(f"ada{n}_loaded") for n in range(2)]
        ada_count = [0]
        ada_free = [[], []]
        silu_ready = act(silu_c[:, :], columns[:, COLUMN_AT["c_2"]:COLUMN_AT["c_2"] + KT], ACT.Silu, [])

        def modulation_vector(v, result_free):
            got = None
            for k in range(KT):
                n = ada_count[0]
                ada_count[0] += 1
                s = n % 2
                loaded = load(ada[s][:, :], dram["w_ada"][k * P:(k + 1) * P, v * D:(v + 1) * D], ada_sems[s],
                              16 * (n // 2 + 1), ada_free[s])
                if k == 0:
                    got = ts(ada_sum[:, :], ada[s][:, :], silu_c[:, 0:1], None, ALU.mult, None,
                             [loaded, silu_ready, *result_free], engine="pool")
                else:
                    scaled = ts(ada[s][:, :], ada[s][:, :], silu_c[:, k:k + 1], None, ALU.mult, None,
                                [loaded, silu_ready], engine="pool")
                    got = tt(ada_sum[:, :], ada_sum[:, :], ada[s][:, :], ALU.add, [scaled, got], engine="pool")
                ada_free[s] = [got]
                yield
                yield
            vector_sum[0] = got

        vector_sum = [None]
        mod_ready = {}

        def modulation_columns():
            free = []
            for v in range(6):
                yield from modulation_vector(v, free)
                for _ in range(6):
                    yield
                bank, bank_free = yield from slot(stat_bank)
                for k in range(KT):
                    summed = mm(bank[:, k:k + 1], ada_sum[:, k * P:(k + 1) * P], ones_all[:, 0:1], True, True,
                                [vector_sum[0], *bank_free] if k == 0 else (), signal=k == KT - 1)
                at = COLUMN_AT["b_ada_2"] + v * KT
                mod_ready[v] = tt(mod[:, v, :], bank[:, 0:KT], columns[:, at:at + KT], ALU.add, [summed])
                stat_bank.put(bank, [mod_ready[v]])
                free = [summed]

        def rms_rows(source, sem, rows_loaded, count, stack, name):
            tiles = [place(stack, f"{name}{t}", [P, D]) for t in range(count)]
            ready = []
            for t in range(count):
                loaded = load(tiles[t][:, :], source[t * P:(t + 1) * P, :], sem, rows_loaded + 16 * (t + 1))
                loads.append(loaded)
            for t in range(count):
                sq, free = scratch.get()
                squares, total = small_columns(2), small_columns()
                waits = [loads[-1], *free]
                got = act(sq[:, :], tiles[t][:, 0:512], ACT.Square, waits, accum=squares[:, 0:1])
                got = act(sq[:, :], tiles[t][:, 512:1024], ACT.Square, [got], accum=squares[:, 1:2])
                scratch.put(sq, [got])
                summed = tt(total, squares[:, 0:1], squares[:, 1:2], ALU.add, [got])
                r = small_columns()
                got = rsqrt_column(r, total, 1.0 / D, EPS6, [summed])
                ready.append([ts(tiles[t][:, :], tiles[t][:, :], r, None, ALU.mult, None, [got])])
            return tiles, ready

        loads = []
        sem_x = semaphore("x_loaded")
        with ExitStack() as phase:
            tiles, ready = rms_rows(dram["x"], sem_x, 0, TT, phase, "x_rows")
            start_weights()
            h_ready = turn_scaled(tiles, ready, *h_T, lambda k: column("norm_g", k), TT, [])
        fence = q.latest()

        def project(n, y_first, branch_waits):
            gates = []
            for step in range(KT + MERGE_LEAD):
                if step < KT:
                    bank, done = feature_unit(f"merge{n}.{step}", h_T)
                    gate, free = scratch.get(tick)
                    gated = act(gate[:, :], bank[:, :], ACT.Sigmoid, [done, *free])
                    unit_banks.put(bank, [gated])
                    gates.append((gate, gated))
                if step < MERGE_LEAD:
                    continue
                d = step - MERGE_LEAD
                waits = branch_waits() if d == 0 else ()
                gate, gated = gates[d]
                bank, done = feature_unit(f"proj{n}.{d}", branch, waits=waits)
                if y_first:
                    y_last[d] = tt(y_T[:, d, :], bank[:, :], gate[:, :], ALU.mult, [done, gated])
                    unit_banks.put(bank, [y_last[d]])
                else:
                    product = tt(gate[:, :], bank[:, :], gate[:, :], ALU.mult, [done, gated])
                    unit_banks.put(bank, [product])
                    y_last[d] = tt(y_T[:, d, :], y_T[:, d, :], gate[:, :], ALU.add, [product, y_last[d]])
                scratch.put(gate, [y_last[d]])
            return done

        y_last = [None] * KT
        branch_free = []

        with ExitStack() as phase:
            PAD = CONV_K - 1
            padded = [place(phase, f"conv_in{n}", [P, PAD + S]) for n in range(2)]
            conv = place(phase, "conv_out", [P, KT, S])
            pads = [pool(lambda e, n=n: e.memset(padded[n][:, 0:PAD], 0.0), fence) for n in range(2)]
            q.wait("dve", fence)
            padded_slots = Slots(padded)
            conv_ready = [None] * KT

            shares = [place(phase, f"conv_share{n}", [P, S]) for n in range(2)]
            products = Slots([place(phase, f"conv_product{n}", [P, S]) for n in range(3)])
            conv_gates = place(phase, "conv_gates", [P, KT, S])
            conv_gated = [None] * KT
            VECTOR_TAPS = 20
            share_free = [[], []]

            def taps(n, u, ready):
                weight = lambda j: columns[:, COLUMN_AT["conv_dw"] + j * KT + n:COLUMN_AT["conv_dw"] + j * KT + n + 1]
                share = shares[n % 2]
                last_share = None
                got = ts(conv[:, n, :], u[:, 0:S], weight(0), column("conv_dw_b", n), ALU.mult, ALU.add, [ready])
                others = list(range(VECTOR_TAPS, CONV_K))
                for j in range(1, VECTOR_TAPS):
                    got = stt(conv[:, n, :], u[:, j:j + S], weight(j), conv[:, n, :], ALU.mult, ALU.add, [got])
                    if j % 2 and others:
                        k = others.pop(0)
                        if last_share is None:
                            last_share = act(share[:, :], u[:, k:k + S], ACT.Copy, [ready, *share_free[n % 2]], scale=weight(k))
                        else:
                            t, free = yield from slot(products)
                            scaled = act(t[:, :], u[:, k:k + S], ACT.Copy, [ready, *free], scale=weight(k))
                            last_share = tt(share[:, :], share[:, :], t[:, :], ALU.add, [scaled, last_share], engine="pool")
                            products.put(t, [last_share])
                    if j % 5 == 4:
                        yield
                for k in others:
                    t, free = yield from slot(products)
                    scaled = act(t[:, :], u[:, k:k + S], ACT.Copy, [ready, *free], scale=weight(k))
                    last_share = tt(share[:, :], share[:, :], t[:, :], ALU.add, [scaled, last_share], engine="pool")
                    products.put(t, [last_share])
                padded_slots.put(u, [got, scaled])
                yield
                conv_ready[n] = tt(conv[:, n, :], conv[:, n, :], share[:, :], ALU.add, [got, last_share])
                share_free[n % 2] = [conv_ready[n]]

            for n in range(KT):
                bank_b, done_b = feature_unit(f"conv_b.{n}", h_T, waits=h_ready)
                gate, free = scratch.get(tick)
                gated = act(gate[:, :], bank_b[:, :], ACT.Sigmoid, [done_b, *free])
                unit_banks.put(bank_b, [gated])
                bank_a, done_a = feature_unit(f"conv_a.{n}", h_T)
                u, free = padded_slots.get(tick)
                got = tt(u[:, PAD:PAD + S], bank_a[:, :], gate[:, :], ALU.mult, [done_a, gated, *free, *pads])
                unit_banks.put(bank_a, [got])
                scratch.put(gate, [got])
                spawn(taps(n, u, got))
                bank, done = feature_unit(f"conv_gate.{n}", h_T)
                conv_gated[n] = act(conv_gates[:, n, :], bank[:, :], ACT.Silu, [done])
                unit_banks.put(bank, [conv_gated[n]])

            def conv_norm():
                while None in conv_ready:
                    yield
                bank, free = stat_bank.get()
                for n in range(KT):
                    summed = mm(bank[:, :], ones_all[:, :], conv[:, n, :], n == 0, n == KT - 1,
                                [conv_ready[n], *free], signal=n == KT - 1)
                centred = []
                for n in range(KT):
                    centred.append(stt(conv[:, n, :], bank[:, :], -1.0 / D, conv[:, n, :], ALU.mult, ALU.add, [summed]))
                stat_bank.put(bank, [centred[-1]])
                bank, free = side_banks.get()
                for n in range(KT):
                    sq, sq_free = scratch.get()
                    squared = act(sq[:, :], conv[:, n, :], ACT.Square, [centred[n], *sq_free])
                    summed = mm(bank[:, :], ones_all[:, :], sq[:, :], n == 0, n == KT - 1, [squared, *free], signal=True)
                    scratch.put(sq, [summed])
                r, got_ln, got = rsqrt_rows(bank[:, :], [summed], D, EPS5)
                side_banks.put(bank, [got_ln])
                for n in range(KT):
                    conv_ready[n] = tt(conv[:, n, :], conv[:, n, :], r[:, :], ALU.mult, [got, centred[n]])
                scratch.put(r, [conv_ready[-1]])

            def conv_finish():
                yield from conv_norm()
                for n in range(KT):
                    normed, free = yield from slot(scratch)
                    got = act(normed[:, :], conv[:, n, :], ACT.Silu, [conv_ready[n], *free], bias=column("conv_ln_b", n),
                              scale=column("conv_ln_g", n))
                    got = tt(normed[:, :], normed[:, :], conv_gates[:, n, :], ALU.mult, [got, conv_gated[n]])
                    both = split(branch[0][:, n, :], branch[1][:, n, :], normed[:, :], [got])
                    scratch.put(normed, both)
                    branch_ready.extend(both)

            branch_ready = []
            conv_task = spawn(conv_finish())

            def conv_waits():
                finish(conv_task)
                return branch_ready[-2:]

            last_product = project(0, True, conv_waits)
            ada_task = spawn(modulation_columns())
            branch_free = [last_product]
        fence = q.latest()

        with ExitStack() as phase:
            k_x = pair(phase, "k_x", [P, KT, M])
            v_x = pair(phase, "v_x", [P, M // P, D])
            for engine in ("act", "dve"):
                q.wait(engine, fence)
            with ExitStack() as inner:
                mem_T = pair(inner, "mem_T", [P, KT, M])
                with ExitStack() as rows:
                    q.wait("sync", fence)
                    tiles, ready = rms_rows(dram["mem"], sem_x, 16 * TT, M // P, rows, "mem_rows")
                    mem_ready = turn_scaled(tiles, ready, *mem_T, lambda k: column("mem_norm_g", k), M // P, [])

                def finish_norm(parts_in, ones, size, gains, outs, width, record, out_free=()):
                    squares = []
                    for bank, done in parts_in:
                        sq, free = yield from slot(scratch)
                        squares.append((sq, act(sq[:, 0:width], bank[:, 0:width], ACT.Square, [done, *free])))
                    yield
                    stat, free = yield from slot(stat_bank)
                    for n, (sq, squared) in enumerate(squares):
                        summed = mm(stat[:, 0:width], ones[:, :], sq[:, 0:width], n == 0, n == len(squares) - 1,
                                    [squared, *free], signal=True)
                        scratch.put(sq, [summed])
                    yield
                    r, free = yield from slot(scratch)
                    got_ln = act(r[:, 0:width], stat[:, 0:width], ACT.Ln, [summed, *free], bias=EPS6, scale=1.0 / size)
                    got = act(r[:, 0:width], r[:, 0:width], ACT.Exp, [got_ln], scale=-0.5)
                    stat_bank.put(stat, [got_ln])
                    full, free = yield from slot(scratch)
                    for (bank, done), gain, (hi, lo) in zip(parts_in, gains, outs):
                        scaled = stt(full[:, 0:width], bank[:, 0:width], gain, r[:, 0:width], ALU.mult, ALU.mult,
                                     [got, *free])
                        unit_banks.put(bank, [scaled])
                        both = split(hi, lo, full[:, 0:width], [scaled, *out_free])
                        free = both
                        record += both
                    scratch.put(r, [scaled])
                    scratch.put(full, both)

                k_tokens = []
                task = None
                for h in range(X_HEADS):
                    held = []
                    for c in range(2):
                        held.append(feature_unit(f"xk.{2 * h + c}", mem_T, width=M, waits=mem_ready))
                    if task is not None:
                        finish(task)
                    task = spawn(finish_norm(held, ones_all, X_DIM, [column("x_kn_g", c) for c in range(2)],
                                             [(k_x[0][:, 2 * h + c, :], k_x[1][:, 2 * h + c, :]) for c in range(2)],
                                             M, k_tokens))
                    tick()
                v_tokens = []
                finish(task)
                for half in range(2):
                    held = [side_banks.get() for _ in range(M // P)]
                    done = token_units(f"xv{half}", mem_T, M // P, [b for b, _ in held], [f for _, f in held])
                    cols = slice(half * 512, (half + 1) * 512)
                    for t, (bank, _) in enumerate(held):
                        both = split(v_x[0][:, t, cols], v_x[1][:, t, cols], bank[:, :], [done[t]])
                        side_banks.put(bank, both)
                        v_tokens += both
                inner_fence = q.latest()

            q_x = [pair(phase, f"q_x{n}", [P, 2, S]) for n in range(2)]
            p_T = pair(phase, "p_T", [P, M // P, S])
            for engine in ("act", "dve"):
                q.wait(engine, inner_fence)
            x_gain = place(phase, "x_gain", [P, 2])
            x_gain_ready = ts(x_gain[:, :], columns[:, COLUMN_AT["x_qn_g"]:COLUMN_AT["x_qn_g"] + 2], X_DIM ** -0.5, None,
                              ALU.mult, None, [])
            q.wait("dve", [x_gain_ready])
            q_free = [[], []]
            p_T_free = []

            def cross_attention(h, q_pair, q_tokens, gates):
                nonlocal p_T_free
                p_tokens = []
                held = None
                for t in range(TT + 1):
                    if t < TT:
                        scores, free = side_banks.get()
                        for c in range(2):
                            qs = slice(t * P, (t + 1) * P)
                            done = mm3(scores[:, 0:M], (q_pair[0][:, c, qs], q_pair[1][:, c, qs]),
                                       (k_x[0][:, 2 * h + c, :], k_x[1][:, 2 * h + c, :]), c == 0, c == 1,
                                       [*q_tokens, *k_tokens, *free], signal=c == 1)
                        top, total, inverse = small_columns(), small_columns(), small_columns()
                        got = dve(lambda e, top=top, scores=scores: e.tensor_reduce(
                            top, scores[:, 0:M], AX, ALU.max, negate=True), [done])
                        p, free = scratch.get()
                        got = act(p[:, 0:M], scores[:, 0:M], ACT.Exp, [got, *free], bias=top, accum=total)
                        side_banks.put(scores, [got])
                        got = dve(lambda e, inverse=inverse, total=total: e.reciprocal(inverse, total), [got])
                        ready = ts(p[:, 0:M], p[:, 0:M], inverse, None, ALU.mult, None, [got])
                    if held is not None:
                        turned, free = side_banks.get()
                        before, before_ready, u = held
                        for j in range(M // P):
                            done = transpose(turned[:, j * P:(j + 1) * P], before[:, j * P:(j + 1) * P],
                                             [before_ready, *free], signal=j == M // P - 1)
                        scratch.put(before, [done])
                        qs = slice(u * P, (u + 1) * P)
                        grid = turned[:, 0:M].rearrange("p (j c) -> p j c", c=P)
                        both = split(p_T[0][:, :, qs], p_T[1][:, :, qs], grid, [done, *p_T_free])
                        side_banks.put(turned, both)
                        p_tokens += both
                    held = (p, ready, t) if t < TT else None
                    yield
                q_free[h % 2] = [done]
                for c in range(2):
                    o, free = side_banks.get()
                    for j in range(M // P):
                        cols = slice(h * X_DIM + c * P, h * X_DIM + (c + 1) * P)
                        done = mm3(o[:, :], (v_x[0][:, j, cols], v_x[1][:, j, cols]), (p_T[0][:, j, :], p_T[1][:, j, :]),
                                   j == 0, j == M // P - 1, [*p_tokens, *v_tokens, *free], signal=j == M // P - 1)
                    p_T_free = [done]
                    while gates[c] is None:
                        yield
                    gate, gated = gates[c]
                    got = tt(gate[:, :], o[:, :], gate[:, :], ALU.mult, [done, gated])
                    side_banks.put(o, [got])
                    both = split(branch[0][:, 2 * h + c, :], branch[1][:, 2 * h + c, :], gate[:, :], [got, *branch_free])
                    scratch.put(gate, both)
                    branch_tokens.extend(both)
                    yield

            branch_tokens = []
            task = None
            for h in range(X_HEADS):
                held = [feature_unit(f"xq.{2 * h + c}", h_T) for c in range(2)]
                q_tokens = []
                gains = [x_gain[:, c:c + 1] for c in range(2)]
                norm = spawn(finish_norm(held, ones_all, X_DIM, gains,
                                         [(q_x[h % 2][0][:, c, :], q_x[h % 2][1][:, c, :]) for c in range(2)],
                                         S, q_tokens, q_free[h % 2]))
                tick()
                gates = [None, None]
                for c in range(2):
                    bank, done = feature_unit(f"x_gate.{2 * h + c}", h_T)
                    gate, free = scratch.get(tick)
                    gated = act(gate[:, :], bank[:, :], ACT.Silu, [done, *free])
                    unit_banks.put(bank, [gated])
                    gates[c] = (gate, gated)
                finish(norm)
                if task is not None:
                    finish(task)
                task = spawn(cross_attention(h, q_x[h % 2], q_tokens, gates))

            def cross_waits():
                finish(task)
                return branch_tokens[-2:]

            branch_free = [project(1, False, cross_waits)]
        fence = q.latest()

        with ExitStack() as phase:
            distance = place(phase, "distance", [P, S])
            bias = [place(phase, f"bias{n}", [P, S]) for n in range(2)]
            q_d = [pair(phase, f"q_d{n}", [P, S]) for n in range(2)]
            k_d = [pair(phase, f"k_d{n}", [P, S]) for n in range(2)]
            v_d = pair(phase, "v_d", [P, TT, 512])
            a_T = [pair(phase, f"a_T{j}_", [P, S - j * P]) for j in range(TT)]
            lam_in = place(phase, "lam_in", [P, 4, HALF])
            lam = place(phase, "lam", [P, 8])
            for engine in ("act", "dve", "pool"):
                q.wait(engine, fence)
            sem_lam = semaphore("lambda_loaded")
            for n, name in enumerate(("lambda_q1", "lambda_k1", "lambda_q2", "lambda_k2")):
                loaded = load(lam_in[:, n, :], dram[name].broadcast_to([P, HALF]), sem_lam, 16 * (n + 1), fence)
            for n in range(2):
                got = tt(lam_in[:, 2 * n, :], lam_in[:, 2 * n, :], lam_in[:, 2 * n + 1, :], ALU.mult, [loaded])
                got = dve(lambda e, n=n: e.tensor_reduce(lam[:, n:n + 1], lam_in[:, 2 * n, :], AX, ALU.add), [got])
            got = act(lam[:, 2:4], lam[:, 0:2], ACT.Exp, [got])
            got = tt(lam[:, 4:5], lam[:, 3:4], lam[:, 2:3], ALU.subtract, [got])
            minus_lam_ready = ts(lam[:, 5:6], lam[:, 4:5], -LAMBDA_INIT, None, ALU.add, None, [got])
            minus_lam = lam[:, 5:6]
            got = pool(lambda e: e.iota(distance[:, :], pattern=[[1, S]], base=-(S - P), channel_multiplier=-1,
                                        allow_small_or_imprecise_dtypes=True), [])
            distance_ready = pool(lambda e: e.affine_select(
                out=distance[:, :], in_=distance[:, :], pattern=[[-1, S]], compare_op=ALU.is_ge, fill=MASKED,
                base=S - P, channel_multiplier=1), [got])
            q_gain = lam[:, 6:7]
            o_gain = lam[:, 7:8]
            ts(q_gain, column("diff_qn_g"), HALF ** -0.5, None, ALU.mult, None, [])
            gains_ready = ts(o_gain, column("diff_subln_g"), 1.0 - LAMBDA_INIT, None, ALU.mult, None, [])
            q.wait("dve", [gains_ready])
            bias_free = [[], []]
            qk_free = [[], []]
            a_T_free = []
            v_free = []
            v_tokens = []
            branch_tokens = []

            scores_made, values_made = [0], [0]

            def differential_attention(h, qk_tokens, gate_box, v_waits):
                nonlocal a_T_free, v_free
                (q_hi, q_lo), (k_hi, k_lo) = q_d[h % 2], k_d[h % 2]
                slope = 2.0 ** (-8.0 * (h + 1) / HEADS)
                biased = ts(bias[h % 2][:, :], distance[:, :], slope, None, ALU.mult, None,
                            [distance_ready, *bias_free[h % 2]], engine="pool")
                a_tokens = []
                exps, mixed, turned_banks = {}, {}, {}
                for step in range(TT + 3):
                    if step >= 3:
                        u = step - 3
                        while values_made[0] < h:
                            yield
                        turned, done = turned_banks.pop(u)
                        cols = [slice((u - j) * P, (u - j + 1) * P) for j in range(u + 1)]
                        for j in range(u + 1):
                            got = copy(a_T[j][0][:, cols[j]], turned[:, j * P:(j + 1) * P], [done, *a_T_free])
                        for j in range(u + 1):
                            both = [got, tt(a_T[j][1][:, cols[j]], turned[:, j * P:(j + 1) * P],
                                            view(a_T[j][0][:, cols[j]]), ALU.subtract, [got])]
                        side_banks.put(turned, both)
                        a_tokens += both
                    if 2 <= step < TT + 2:
                        u = step - 2
                        s0, ready = mixed.pop(u)
                        turned, free = yield from slot(side_banks)
                        for j in range(u + 1):
                            done = transpose(turned[:, j * P:(j + 1) * P], s0[:, j * P:(j + 1) * P], [ready, *free],
                                             signal=j == u)
                        scratch.put(s0, [done])
                        turned_banks[u] = (turned, done)
                    if 1 <= step < TT + 1:
                        u = step - 1
                        n = (u + 1) * P
                        s0, s1, totals, done_exp = exps.pop(u)
                        inverse, second = small_columns(2), small_columns()
                        got = dve(lambda e, inverse=inverse, totals=totals: e.reciprocal(inverse, totals), [done_exp])
                        c1 = ts(second, inverse[:, 1:2], minus_lam, None, ALU.mult, None, [got, minus_lam_ready])
                        got = ts(s0[:, 0:n], s0[:, 0:n], inverse[:, 0:1], None, ALU.mult, None, [got])
                        ready = stt(s0[:, 0:n], s1[:, 0:n], second, s0[:, 0:n], ALU.mult, ALU.add, [got, c1])
                        scratch.put(s1, [ready])
                        mixed[u] = (s0, ready)
                    if step < TT:
                        n = (step + 1) * P
                        qs = slice(step * P, (step + 1) * P)
                        tops, totals, minus = small_columns(2), small_columns(2), small_columns(2)
                        ps = []
                        for m in range(2):
                            rows = slice(m * HALF, (m + 1) * HALF)
                            scores, free = yield from slot(side_banks)
                            done = mm3(scores[:, 0:n], (q_hi[rows, qs], q_lo[rows, qs]), (k_hi[rows, 0:n], k_lo[rows, 0:n]),
                                       True, True, [*qk_tokens, *free], signal=True)
                            s, free = yield from slot(scratch)
                            got = dve(lambda e, s=s, scores=scores, m=m, n=n, tops=tops: e.tensor_tensor_reduce(
                                out=s[:, 0:n], in0=scores[:, 0:n], in1=bias[h % 2][:, S - n:S], scale=1.0,
                                scalar=MASKED, op0=ALU.add, op1=ALU.max, accum_out=tops[:, m:m + 1]),
                                [done, biased, *free])
                            side_banks.put(scores, [got])
                            ps.append(s)
                        last_scores = done
                        got = ts(minus, tops, -1.0, None, ALU.mult, None, [got])
                        for m in range(2):
                            done_exp = act(ps[m][:, 0:n], ps[m][:, 0:n], ACT.Exp, [got], bias=minus[:, m:m + 1],
                                           accum=totals[:, m:m + 1])
                        exps[step] = (ps[0], ps[1], totals, done_exp)
                        if step == TT - 1:
                            bias_free[h % 2] = [got]
                            qk_free[h % 2][:] = [last_scores]
                            scores_made[0] = h + 1
                    yield
                o, free = yield from slot(side_banks)
                cols = slice((h % 4) * P, (h % 4 + 1) * P)
                for j in range(TT):
                    done = mm3(o[:, j * P:S], (v_d[0][:, j, cols], v_d[1][:, j, cols]), (a_T[j][0][:, :], a_T[j][1][:, :]),
                               j == 0, j == TT - 1, [*a_tokens, *v_waits, *free], signal=j == TT - 1)
                a_T_free = [done]
                v_free = [done]
                values_made[0] = h + 1
                sq, free = yield from slot(scratch)
                squared = act(sq[:, :], o[:, :], ACT.Square, [done, *free])
                yield
                stat, free = yield from slot(stat_bank)
                summed = mm(stat[:, :], ones_all[:, :], sq[:, :], True, True, [squared, *free], signal=True)
                yield
                got_ln = act(sq[:, :], stat[:, :], ACT.Ln, [summed], bias=EPS6, scale=1.0 / P)
                got = act(sq[:, :], sq[:, :], ACT.Exp, [got_ln], scale=-0.5)
                stat_bank.put(stat, [got_ln])
                while gate_box[0] is None:
                    yield
                gate, gated = gate_box[0]
                got = stt(sq[:, :], o[:, :], o_gain, sq[:, :], ALU.mult, ALU.mult, [got])
                side_banks.put(o, [got])
                got = tt(gate[:, :], gate[:, :], sq[:, :], ALU.mult, [got, gated])
                scratch.put(sq, [got])
                both = split(branch[0][:, h, :], branch[1][:, h, :], gate[:, :], [got, *branch_free])
                scratch.put(gate, both)
                branch_tokens.extend(both)

            def norm_qk(h, bank, done, gain, hi, lo, record):
                while scores_made[0] < h - 1:
                    yield
                yield from finish_norm([(bank, done)], ones_head, HALF, [gain], [(hi, lo)], S, record, qk_free[h % 2])

            extra = [place(phase, f"scratch_more{n}", [P, S]) for n in range(3)]
            for t in extra:
                scratch.put(t, [])
            attention = None
            for h in range(HEADS):
                qk_tokens = []
                bank, done = feature_unit(f"dq.{h}", h_T)
                norm_q = spawn(norm_qk(h, bank, done, q_gain, q_d[h % 2][0][:, :], q_d[h % 2][1][:, :], qk_tokens))
                bank, done = feature_unit(f"dk.{h}", h_T)
                norm_k = spawn(norm_qk(h, bank, done, column("diff_kn_g"), k_d[h % 2][0][:, :], k_d[h % 2][1][:, :],
                                       qk_tokens))
                tick()
                if h % 4 == 0:
                    if attention is not None:
                        finish(attention)
                    held = [side_banks.get(tick) for _ in range(TT)]
                    done = token_units(f"dv{h // 4}", h_T, TT, [b for b, _ in held], [f for _, f in held])
                    v_tokens = []
                    for t, (bank, _) in enumerate(held):
                        both = split(v_d[0][:, t, :], v_d[1][:, t, :], bank[:, :], [done[t], *v_free])
                        side_banks.put(bank, both)
                        v_tokens += both
                gate_box = [None]
                bank, done = feature_unit(f"d_gate.{h}", h_T)
                gate, free = scratch.get(tick)
                gated = act(gate[:, :], bank[:, :], ACT.Silu, [done, *free])
                unit_banks.put(bank, [gated])
                gate_box[0] = (gate, gated)
                finish(norm_q)
                finish(norm_k)
                attention = spawn(differential_attention(h, qk_tokens, gate_box, v_tokens))

            def differential_waits():
                finish_all()
                return branch_tokens[-2:]

            last = project(2, False, differential_waits)
            finish_all()
            scratch.ready = [(t, free) for t, free in scratch.ready if all(t is not x for x in extra)]
        finish_all()

        y_tokens = []
        for d in range(KT):
            y_tokens += split(h_T[0][:, d, :], h_T[1][:, d, :], y_T[:, d, :], [y_last[d], last])
        sem_res = semaphore("x_again_loaded")
        for t in range(TT):
            loaded = load(x_rows[t], dram["x"][t * P:(t + 1) * P, :], sem_res, 16 * (t + 1), y_tokens[-2:])
        x_ready = [None] * TT

        def token_projection(label, x, waits, consume):
            for half in range(2):
                held = [side_banks.get(tick) for _ in range(TT)]
                done = token_units(f"{label}{half}", x, TT, [b for b, _ in held], [f for _, f in held], waits=waits)
                for t, (bank, _) in enumerate(held):
                    side_banks.put(bank, [consume(t, slice(half * 512, (half + 1) * 512), bank, done[t])])

        def add_residual(t, cols, bank, done):
            x_ready[t] = tt(x_rows[t][:, cols], x_rows[t][:, cols], bank[:, :], ALU.add, [done, loaded])
            return x_ready[t]

        token_projection("w_out", h_T, y_tokens[-2:], add_residual)
        first.close()
        fence = q.latest()

        fold = place(whole, "fold", [P, 4, KT])
        one_minus_ka = place(whole, "one_minus_ka", [P, MIX // P])
        for engine in ("act", "dve", "pool"):
            q.wait(engine, fence)

        def vector_columns(name, n=KT):
            return columns[:, COLUMN_AT[name]:COLUMN_AT[name] + n]

        def fold_modulation(n, gain, shift, shift_v, scale_v):
            g, b = fold[:, 2 * n, :], fold[:, 2 * n + 1, :]
            got = stt(g, mod[:, scale_v, :], 1.0, vector_columns(gain), ALU.add, ALU.mult, [mod_ready[scale_v]])
            got = stt(b, mod[:, scale_v, :], 1.0, vector_columns(shift), ALU.add, ALU.mult, [mod_ready[scale_v]])
            return tt(b, b, mod[:, shift_v, :], ALU.add, [got, mod_ready[shift_v]])

        folded = [fold_modulation(0, "emb_ln_g_2", "emb_ln_b_2", 0, 1), fold_modulation(1, "ln1_g_2", "ln1_b_2", 3, 4)]
        ts(one_minus_ka[:, :], vector_columns("k_a_2", MIX // P), -1.0, 1.0, ALU.mult, ALU.add, [])

        def normalise_rows(rows, width, eps_column, waits, out=None):
            pieces = width // 512
            stats = small_columns(6 * pieces)
            for n in range(pieces):
                got = dve(lambda e, n=n: e.bn_stats(stats[:, 6 * n:6 * n + 6], rows[:, n * 512:(n + 1) * 512]), waits)
            aggregate, r = small_columns(2), small_columns()
            got = dve(lambda e: e.bn_aggr(aggregate, stats), [got])
            got = rsqrt_column(r, aggregate[:, 1:2], 1.0, eps_column, [got])
            return ts(rows if out is None else out, rows, aggregate[:, 0:1], r, ALU.subtract, ALU.mult, [got])

        def load_rows(label, pieces):
            sem = semaphore(f"{label}_loaded")
            held = []
            for n, source in enumerate(pieces):
                t, free = scratch.get(tick)
                token = load(t[:, 0:source.shape[1]], source.broadcast_to([P, source.shape[1]]), sem, 16 * (n + 1), free)
                held.append(t)
            return held, token

        def gain_and_shift(label, gain, shift, waits):
            for half in range(2):
                cols = slice(half * 512, (half + 1) * 512)
                (g, b), there = load_rows(f"{label}{half}", [dram[gain][:, cols], dram[shift][:, cols]])
                for t in range(TT):
                    got = tt(x_rows[t][:, cols], x_rows[t][:, cols], g[:, :], ALU.mult, [there, *waits])
                    x_ready[t] = tt(x_rows[t][:, cols], x_rows[t][:, cols], b[:, :], ALU.add, [got])
                scratch.put(g, [got])
                scratch.put(b, [x_ready[-1]])

        def gate_rows(v):
            held = []
            for half in range(2):
                bank, free = side_banks.get(tick)
                diagonal, diagonal_free = scratch.get(tick)
                for n in range(4):
                    k = 4 * half + n
                    built = ts(diagonal[:, n * P:(n + 1) * P], ident[:, :], mod[:, v, k:k + 1], None, ALU.mult, None,
                               [mod_ready[v], *diagonal_free])
                done = mm(bank[:, :], ones_all[:, :], diagonal[:, :], True, True, [built, *free], signal=True)
                got = copy(diagonal[:, :], bank[:, :], [done])
                side_banks.put(bank, [got])
                held.append((diagonal, got))
            return held

        def modulated_residual(v, label, x, waits, project_it):
            gates = gate_rows(v)

            def consume(t, cols, bank, done):
                gate, gate_ready = gates[cols.start // 512]
                product, free = scratch.get(tick)
                moved = tt(product[:, :], bank[:, :], gate[:, :], ALU.mult, [done, gate_ready, *free])
                x_ready[t] = stt(x_rows[t][:, cols], x_rows[t][:, cols], ALPHA, product[:, :], ALU.mult, ALU.add,
                                 [moved, x_ready[t]])
                scratch.put(product, [x_ready[t]])
                return moved

            project_it(label, x, waits, consume)
            for gate, _ in gates:
                scratch.put(gate, [x_ready[-1]])

        for t in range(TT):
            x_ready[t] = normalise_rows(x_rows[t], D, EPS5, [x_ready[t]])

        mixed_stack = ExitStack()
        FW = MIX // P
        y_a = pair(mixed_stack, "y_a", [P, FW, S])
        second = ExitStack()
        AR = place(second, "AR", [P, FW, 2, S])
        k_T = place(second, "k_T", [P, FW, S])
        v_T = place(second, "v_T", [P, FW, S])
        lora_in = place(second, "lora_in", [P, S])
        gd_T = place(second, "gd_T", [P, 2, S])
        with ExitStack() as phase:
            h2_T = pair(phase, "h2_T", [P, KT, S])
            u_T = place(phase, "u_T", [P, MIX // P, S])
            v_sg = pair(phase, "v_sg", [P, MIX])
            w_s = place(phase, "w_s", [P, 4 * P])
            w_sp = pair(phase, "w_sp", [P, 4 * P])
            shifted = [place(phase, f"shifted{n}", [P, 1 + S]) for n in range(2)]
            h2_ready = turn_scaled(x_rows, [[x_ready[t]] for t in range(TT)], *h2_T, lambda k: fold[:, 0, k:k + 1], TT,
                                   folded, lambda k: fold[:, 1, k:k + 1])
            gain_and_shift("emb_ln", "emb_ln_g", "emb_ln_b", h2_ready)

            sem_ws = semaphore("w_s_loaded")
            loaded = load(w_s[:, :], dram["w_s"].rearrange("s g t -> s (g t)"), sem_ws, 16, fence)
            kept = pool(lambda e: e.affine_select(out=w_s[:, :], in_=w_s[:, :], pattern=[[0, 4], [1, P]],
                                                  compare_op=ALU.is_ge, fill=0.0, base=0, channel_multiplier=-1), [loaded])
            w_sp_ready = split(w_sp[0][:, :], w_sp[1][:, :], w_s[:, :], [kept])
            pads = [pool(lambda e, n=n: e.memset(shifted[n][:, 0:1], 0.0), []) for n in range(2)]

            u_ready = []
            for n in range(4):
                bank, done = feature_unit(f"pu.{n}", h2_T, waits=h2_ready)
                u_ready.append(act(u_T[:, n, :], bank[:, :], ACT.Gelu_apprx_tanh, [done]))
                unit_banks.put(bank, [u_ready[-1]])
            held = [side_banks.get(tick) for _ in range(TT)]
            pv_done = token_units("pv", h2_T, TT, [b for b, _ in held], [f for _, f in held])

            branch_tokens = []

            def spatial_gating():
                (g, b, b_s), there = load_rows("sg_ln", [dram["sg_ln_g"], dram["sg_ln_b"], dram["b_s"]])
                v_free = []
                for t, (bank, _) in enumerate(held):
                    v, free = scratch.get()
                    got = act(v[:, :], bank[:, :], ACT.Gelu_apprx_tanh, [pv_done[t], *free])
                    side_banks.put(bank, [got])
                    got = normalise_rows(v[:, :], MIX, EPS5, [got])
                    got = tt(v[:, :], v[:, :], g[:, :], ALU.mult, [got, there])
                    got = tt(v[:, :], v[:, :], b[:, :], ALU.add, [got])
                    both = split(v_sg[0][:, :], v_sg[1][:, :], v[:, :], [got, *v_free])
                    scratch.put(v, both)
                    yield
                    mixed, free = side_banks.get()
                    for n in range(4):
                        cols = slice(n * P, (n + 1) * P)
                        done = mm3(mixed[:, cols], (v_sg[0][:, cols], v_sg[1][:, cols]), (w_sp[0][:, cols], w_sp[1][:, cols]),
                                   True, True, [*both, *w_sp_ready, *free], signal=n == 3)
                    v_free = [done]
                    s, free = scratch.get()
                    tok = slice(t * P, (t + 1) * P)
                    got = tt(s[:, :], mixed[:, :], b_s[:, :], ALU.add, [done, *free])
                    side_banks.put(mixed, [got])
                    s4 = s[:, :].rearrange("p (g c) -> p g c", c=P)
                    got = tt(s4, s4, u_T[:, :, tok], ALU.mult, [got, u_ready[-1]])
                    both = split(y_a[0][:, :, tok], y_a[1][:, :, tok], s4, [got])
                    scratch.put(s, both)
                    branch_tokens.extend(both)
                    yield
                for t in (g, b, b_s):
                    scratch.put(t, both)

            spawn(spatial_gating())
            shifted_slots = Slots(shifted)
            rwkv_ready = []
            for n in range(15):
                bank, done = feature_unit(f"rwkv.{n}", h2_T)
                p, free = shifted_slots.get(tick)
                raw_copy = copy(p[:, 1:1 + S], bank[:, :], [done, *free])
                unit_banks.put(bank, [raw_copy])
                change, free = scratch.get(tick)
                got = tt(change[:, :], p[:, 0:S], p[:, 1:1 + S], ALU.subtract, [raw_copy, *pads, *free])
                if n < 12:
                    target = (AR[:, n % 4, 1, :], k_T[:, n % 4, :], v_T[:, n % 4, :])[n // 4]
                else:
                    target = lora_in[:, :] if n == 12 else gd_T[:, n - 13, :]
                got = stt(target, change[:, :], column("mu_shift_2", n), p[:, 1:1 + S], ALU.mult, ALU.add, [got])
                scratch.put(change, [got])
                shifted_slots.put(p, [got])
                rwkv_ready.append(got)
            finish_all()
            tanh_ready = act(lora_in[0:HALF, :], lora_in[0:HALF, :], ACT.Tanh, [rwkv_ready[12]])
            gd_ready = act(gd_T[:, :, :], gd_T[:, :, :], ACT.Sigmoid, [rwkv_ready[-1]])
        fence = q.latest()

        with ExitStack() as phase:
            lora_w = place(phase, "lora_w", [P, MIX])
            g_up = place(phase, "g_up", [P, 2, MIX])
            keep = place(phase, "keep", [P, S])
            mask = place(phase, "mask", [P, 4, P])
            levels = place(phase, "levels", [P, 6, P])
            feature_sets = Slots([(place(phase, f"Bw{n}", [P, S]),
                                   [place(phase, f"tok{n}{c}", [P, TT, P]) for c in "abkv"]) for n in range(2)])
            chunk_sets = Slots([(place(phase, f"P_T{n}", [P, NC, P]), place(phase, f"Z{n}", [P, NC, P]))
                                for n in range(2)])
            work_sets = Slots([(place(phase, f"LM{n}", [P, 4, 4, P]), place(phase, f"X{n}", [P, 4, P]),
                                place(phase, f"Y{n}", [P, 4, P]), place(phase, f"W{n}", [P, 4, P])) for n in range(2)])
            log2_shift = 20
            for _ in range(3):
                bank, free = unit_banks.get()
                side_banks.put(bank, free)
            for engine in ("act", "dve", "pool"):
                q.wait(engine, fence)
            sem_lora = semaphore("lora_loaded")
            load(lora_w[0:HALF, :], dram["w_up"], sem_lora, 16, fence)
            load(lora_w[HALF:P, :], dram["a_up"], sem_lora, 32)
            load(g_up[:, 0, :], dram["g_up"][0:P, :], sem_lora, 48)
            zeroed = pool(lambda e: e.memset(g_up[:, 1, :], 0.0), [])
            lora_ready = load(g_up[0:32, 1, :], dram["g_up"][P:160, :], sem_lora, 64, [zeroed])
            pool(lambda e: e.memset(keep[:, :], 1.0), [])
            pool(lambda e: e.memset(keep[:, :].rearrange("p (c t) -> p c t", t=CHUNK)[:, :, 0:1], 0.0), [])
            pool(lambda e: e.memset(mask[:, :, :], 1.0), [])
            pool(lambda e: e.memset(mask[0:CHUNK, :, CHUNK:P], 0.0), [])
            for n in range(4):
                pool(lambda e, n=n: e.affine_select(out=mask[:, n, :], in_=mask[:, n, :], pattern=[[1, P]],
                                                    compare_op=ALU.is_gt if n % 2 == 0 else ALU.is_ge, fill=0.0, base=0,
                                                    channel_multiplier=-1), [])
            pool(lambda e: e.memset(levels[:, :, :], 1.0), [])
            for n in range(5):
                size = 2 ** (n + 1)
                pat = [[size, P // size], [0, size]]
                pool(lambda e, n=n, pat=pat: e.affine_select(
                    out=levels[:, n, :], in_=levels[:, n, :], pattern=[[-a, b] for a, b in pat], compare_op=ALU.is_ge,
                    fill=0.0, base=0, channel_multiplier=1), [])
                pool(lambda e, n=n, pat=pat, size=size: e.affine_select(
                    out=levels[:, n, :], in_=levels[:, n, :], pattern=pat, compare_op=ALU.is_ge,
                    fill=0.0, base=size - 1, channel_multiplier=-1), [])
            tt(levels[:, 5, :], ones_head[:, :], levels[:, 4, :], ALU.subtract, [], engine="pool")
            for n in range(4, 0, -1):
                tt(levels[:, n, :], levels[:, n, :], levels[:, n - 1, :], ALU.subtract, [], engine="pool")
            tt(levels[:, 0, :], levels[:, 0, :], ident[:, :], ALU.subtract, [], engine="pool")
            masks_ready = pool(lambda e: e.memset(eps[:, 3:4], 0.5 * log2_shift * math.log(2.0)), [])
            for engine in ("act", "dve", "pe"):
                q.wait(engine, [lora_ready, masks_ready, tanh_ready, gd_ready, rwkv_ready[-1]])

            def four(ap):
                return ap.rearrange("p (o c) -> p o c", o=1).broadcast_to([P, 4, P])

            def grid(ap, c=P):
                return ap.rearrange("p (n c) -> p n c", c=c)

            features_of, chunks_of = [None] * FW, [None] * FW
            halves_done = [0] * FW
            halves_started, y_ready = [0], [None] * FW

            def features(f):
                while f > 0 and features_of[f - 1] is None:
                    yield
                (Bw, turned4), set_free = yield from slot(feature_sets)
                cols = slice(f * P, (f + 1) * P)
                A_f, R_f, K_f, V_f = AR[:, f, 0, :], AR[:, f, 1, :], k_T[:, f, :], v_T[:, f, :]
                bank, free = yield from slot(side_banks)
                done = mm(bank[:, :], lora_w[0:HALF, cols], lora_in[0:HALF, :], True, True, free, signal=True)
                log_w, free = yield from slot(scratch)
                got = act(log_w[:, :], bank[:, :], ACT.Sigmoid, [done, *free], bias=column("w0_2", f))
                side_banks.put(bank, [got])
                bank, free = yield from slot(side_banks)
                done = mm(bank[:, :], lora_w[HALF:P, cols], lora_in[HALF:P, :], True, True, free, signal=True)
                a, free = yield from slot(scratch)
                a_ready = act(a[:, :], bank[:, :], ACT.Sigmoid, [done, *free], bias=column("a0_2", f))
                side_banks.put(bank, [a_ready])
                yield
                scaled = ts(log_w[:, :], log_w[:, :], -math.exp(-0.5), None, ALU.mult, None, [got])
                total, free = yield from slot(scratch)
                summed = dve(lambda e: e.tensor_tensor_scan(
                    total[:, :], keep[:, :], log_w[:, :], 0.0, ALU.mult, ALU.add), [scaled, *free])
                before = tt(log_w[:, :], total[:, :], log_w[:, :], ALU.subtract, [summed])
                w_before = act(log_w[:, :], log_w[:, :], ACT.Exp, [before])
                sq, free = yield from slot(scratch)
                got = act(sq[:, :], K_f, ACT.Square, free, scale=column("k_k_2", f))
                yield
                stat, free = yield from slot(stat_bank)
                done = mm(stat[:, :], ones_head[:, :], sq[:, :], True, True, [got, *free], signal=True)
                clamped = ts(sq[:, :], stat[:, :], 1e-24, None, ALU.max, None, [done])
                stat_bank.put(stat, [clamped])
                yield
                got = act(sq[:, :], sq[:, :], ACT.Ln, [clamped], scale=2.0 ** log2_shift)
                got = act(sq[:, :], sq[:, :], ACT.Exp, [got], scale=-0.5, bias=eps[:, 3:4])
                kk, free = yield from slot(scratch)
                kk_ready = stt(kk[:, :], K_f, column("k_k_2", f), sq[:, :], ALU.mult, ALU.mult, [got, *free])
                yield
                a_done = stt(A_f, kk[:, :], -1.0, log_w[:, :], ALU.mult, ALU.mult, [kk_ready, w_before])
                scratch.put(log_w, [a_done])
                b_ready = tt(kk[:, :], kk[:, :], a[:, :], ALU.mult, [a_done, a_ready])
                got = ts(a[:, :], a[:, :], column("k_a_2", f), one_minus_ka[:, f:f + 1], ALU.mult, ALU.add, [b_ready])
                k_ready = tt(a[:, :], a[:, :], K_f, ALU.mult, [got])
                yield
                got = stt(sq[:, :], R_f, column("r_k_2", f), a[:, :], ALU.mult, ALU.mult, [k_ready, kk_ready])
                w_all, free = yield from slot(scratch)
                w_ready = act(w_all[:, :], total[:, :], ACT.Exp, [summed, *free])
                stat, free = yield from slot(stat_bank)
                bonus_sum = mm(stat[:, :], ones_head[:, :], sq[:, :], True, True, [got, *free], signal=True)
                scratch.put(sq, [bonus_sum])
                r_done = tt(R_f, R_f, w_all[:, :], ALU.mult, [w_ready, got])
                last_w = small_columns(NC)
                ends = grid(w_all[:, :], CHUNK)[:, :, CHUNK - 1:CHUNK]
                last_w_ready = dve(lambda e: e.tensor_copy(grid(last_w, 1), ends), [w_ready])
                yield
                inverse_ready = act(w_all[:, :], total[:, :], ACT.Exp, [r_done, last_w_ready], scale=-1.0)
                tt(Bw[:, :], kk[:, :], w_all[:, :], ALU.mult, [inverse_ready, b_ready, *set_free])
                bk_ready = tt(K_f, a[:, :], w_all[:, :], ALU.mult, [inverse_ready, k_ready])
                by_chunk = grid(total[:, :], CHUNK)
                end_sum = small_columns(NC)
                got = dve(lambda e: e.tensor_copy(grid(end_sum, 1), by_chunk[:, :, CHUNK - 1:CHUNK]), [summed])
                got = tt(grid(w_all[:, :], CHUNK), grid(end_sum, 1).broadcast_to([P, NC, CHUNK]), by_chunk,
                         ALU.subtract, [got, bk_ready])
                scratch.put(total, [got])
                yield
                got = act(w_all[:, :], w_all[:, :], ACT.Exp, [got])
                be_ready = tt(kk[:, :], kk[:, :], w_all[:, :], ALU.mult, [got, bk_ready])
                ke_ready = tt(a[:, :], a[:, :], w_all[:, :], ALU.mult, [got, bk_ready])
                scratch.put(w_all, [ke_ready])
                yield
                turned_ready = []
                for n, (source, ready) in enumerate(((A_f, a_done), (kk[:, :], be_ready), (a[:, :], ke_ready), (V_f, None))):
                    bank, free = yield from slot(side_banks)
                    for i in range(TT):
                        done = transpose(bank[:, i * P:(i + 1) * P], source[:, i * P:(i + 1) * P], [ready, *free],
                                         signal=i == TT - 1)
                    got = copy(turned4[n][:, :, :], grid(bank[:, :]), [done, *set_free])
                    side_banks.put(bank, [got])
                    turned_ready.append(got)
                    yield
                scratch.put(kk, turned_ready)
                scratch.put(a, turned_ready)
                bonus_ready = tt(V_f, stat[:, :], V_f, ALU.mult, [bonus_sum, turned_ready[-1]])
                stat_bank.put(stat, [bonus_ready])
                features_of[f] = (Bw, turned4, [bk_ready, a_done, r_done], turned_ready, last_w, last_w_ready, bonus_ready)

            def chunk_half(f, half):
                while features_of[f] is None or halves_started[0] < 2 * f + half:
                    yield
                if half == 0:
                    chunks_of[f] = yield from slot(chunk_sets)
                (LM, X, Y, W), work_free = yield from slot(work_sets)
                halves_started[0] += 1
                (P_T, Z), chunks_free = chunks_of[f]
                Bw, (A_tok, B_tok, K_tok, V_tok), rows_ready, turned_ready, last_w, last_w_ready, _ = features_of[f]
                G, H, LkV = X[:, 0:2, :], X[:, 2:4, :], grid(W[:, 0:2, :].rearrange("p a b -> p (a b)"), HALF)
                tiles = [2 * half, 2 * half + 1]
                tok2 = slice(2 * half * P, 2 * (half + 1) * P)

                def head(m):
                    return slice((m % 2) * HALF, (m % 2 + 1) * HALF)

                for m in range(4):
                    tok = slice(tiles[m // 2] * P, (tiles[m // 2] + 1) * P)
                    bank, free = yield from slot(side_banks)
                    mm(bank[:, 0:2 * P], Bw[head(m), tok], AR[head(m), f, :, tok], True, True, [*rows_ready, *free])
                    done = mm(bank[:, 2 * P:4 * P], k_T[head(m), f, tok], AR[head(m), f, :, tok], True, True, signal=True)
                    masked = tt(LM[:, m, :, :], grid(bank[:, :]), mask[:, :, :], ALU.mult, [done, *work_free])
                    side_banks.put(bank, [masked])
                    if m % 2:
                        yield
                NT = LM[:, :, 0, :]
                got = tt(Y[:, :, :], NT, four(levels[:, 0, :]), ALU.mult, [masked, *work_free], engine="pool")
                y_done = tt(Y[:, :, :], Y[:, :, :], four(ident[:, :]), ALU.add, [got], engine="pool")
                bt_done = tt(W[:, :, :], NT, four(levels[:, 1, :]), ALU.mult, [masked, *work_free], engine="pool")
                bank, free = yield from slot(side_banks)
                for m in range(4):
                    done = transpose(bank[:, m * P:(m + 1) * P], LM[:, m, 0, :], [masked, *free], signal=m == 3)
                got = tt(X[:, :, :], grid(bank[:, :]), four(levels[:, 0, :]), ALU.mult, [done, *work_free])
                side_banks.put(bank, [got])
                x_done = tt(X[:, :, :], X[:, :, :], four(ident[:, :]), ALU.add, [got])
                yield
                for level in range(1, 6):
                    bank, free = yield from slot(side_banks)
                    for m in range(4):
                        done = mm(bank[:, m * P:(m + 1) * P], W[:, m, :], X[:, m, :], True, True,
                                  [bt_done, x_done, *free], signal=m == 3)
                    yield
                    w_done = copy(W[:, :, :], grid(bank[:, :]), [done])
                    side_banks.put(bank, [w_done])
                    yield
                    bank, free = yield from slot(side_banks)
                    for m in range(4):
                        done = mm(bank[:, m * P:(m + 1) * P], W[:, m, :], Y[:, m, :], True, True,
                                  [w_done, y_done, *free], signal=m == 3)
                    if level < 5:
                        bank_x, free = yield from slot(side_banks)
                        for m in range(4):
                            done_x = mm(bank_x[:, m * P:(m + 1) * P], Y[:, m, :], W[:, m, :], True, True,
                                        free, signal=m == 3)
                        yield
                        y_done = tt(Y[:, :, :], Y[:, :, :], grid(bank[:, :]), ALU.add, [done, done_x])
                        x_done = tt(X[:, :, :], X[:, :, :], grid(bank_x[:, :]), ALU.add, [done_x])
                        side_banks.put(bank_x, [x_done])
                        bt_done = tt(W[:, :, :], NT, four(levels[:, level + 1, :]), ALU.mult, [done_x], engine="pool")
                    else:
                        y_done = tt(Y[:, :, :], Y[:, :, :], grid(bank[:, :]), ALU.add, [done])
                    side_banks.put(bank, [y_done])
                    yield
                bank, free = yield from slot(side_banks)
                for m in range(4):
                    done = mm(bank[:, m * HALF:(m + 1) * HALF], LM[:, m, 2, :], V_tok[:, tiles[m // 2], head(m)], True,
                              True, [*turned_ready, masked, *free], signal=m == 3)
                lkv_ready = copy(LkV, grid(bank[:, 0:4 * HALF], HALF), [done, y_done])
                side_banks.put(bank, [lkv_ready])
                yield
                bank, free = yield from slot(side_banks)
                for m in range(4):
                    mm(bank[:, m * HALF:(m + 1) * HALF], Y[:, m, :], A_tok[:, tiles[m // 2], head(m)], True, True,
                       [y_done, *turned_ready, *free])
                    done = mm(bank[:, (4 + m) * HALF:(5 + m) * HALF], Y[:, m, :], LkV[:, m, :], True, True,
                              [lkv_ready], signal=m == 3)
                yield
                gh_ready = copy(X[:, :, :], grid(bank[:, :]), [done])
                side_banks.put(bank, [gh_ready])
                yield
                bank_q, free_q = yield from slot(side_banks)
                bank_y, free_y = yield from slot(side_banks)
                for m in range(4):
                    rows, at = head(m), slice((m // 2) * P, (m // 2 + 1) * P)
                    mm(bank_q[rows, at], G[:, m // 2, rows], LM[:, m, 1, :], True, True, [gh_ready, *free_q])
                    mm(bank_y[rows, at], H[:, m // 2, rows], LM[:, m, 1, :], True, False, free_y)
                    done = mm(bank_y[rows, at], V_tok[:, tiles[m // 2], rows], LM[:, m, 3, :], False, True,
                              signal=m == 3)
                yield
                q_ready = tt(AR[:, f, 1, tok2], bank_q[:, 0:2 * P], AR[:, f, 1, tok2], ALU.add, [done])
                side_banks.put(bank_q, [q_ready])
                y0_ready = copy(k_T[:, f, tok2], bank_y[:, 0:2 * P], [done])
                side_banks.put(bank_y, [y0_ready])
                for part in range(2):
                    rows = slice(part * CHUNK, (part + 1) * CHUNK)
                    bank, free = yield from slot(side_banks)
                    for n in range(2):
                        i = tiles[n]
                        mm(bank[:, n * P:(n + 1) * P], G[rows, n, :], B_tok[rows, i, :], True, True, free)
                        mm(bank[:, (2 + n) * P:(3 + n) * P], B_tok[rows, i, :], H[rows, n, :], True, False)
                        done = mm(bank[:, (2 + n) * P:(3 + n) * P], K_tok[rows, i, :], V_tok[rows, i, :], False, True,
                                  signal=n == 1)
                    for n in range(2):
                        c = 2 * tiles[n] + part
                        got = tt(P_T[:, c, :], bank[:, n * P:(n + 1) * P], ones_head[:, :], ALU.mult, [done, *chunks_free])
                        z_ready = tt(Z[:, c, :], bank[:, (2 + n) * P:(3 + n) * P], ones_head[:, :], ALU.mult, [done])
                        p_ready = stt(P_T[:, c, :], ident[:, :], last_w[:, c:c + 1], P_T[:, c, :], ALU.mult, ALU.add,
                                      [got, last_w_ready])
                    side_banks.put(bank, [z_ready])
                    yield
                work_sets.put((LM, X, Y, W), [done, p_ready])
                halves_done[f] += 1
                halves_ready[f] += [p_ready, q_ready, y0_ready]
                if halves_done[f] == 2:
                    feature_sets.put((Bw, (A_tok, B_tok, K_tok, V_tok)), [done])

            halves_ready = [[] for _ in range(FW)]

            def states(f):
                while halves_done[f] < 2:
                    yield
                (P_T, Z), _ = chunks_of[f]
                cols = slice(f * P, (f + 1) * P)
                y0, Q_f = k_T[:, f, :], AR[:, f, 1, :]
                state = halves_ready[f][-3]
                for c in range(1, NC - 1):
                    bank, free = yield from slot(side_banks)
                    done = mm(bank[:, 0:P], P_T[:, c, :], Z[:, c - 1, :], True, True, [*halves_ready[f], state, *free],
                              signal=True)
                    state = tt(Z[:, c, :], Z[:, c, :], bank[:, 0:P], ALU.add, [done])
                    side_banks.put(bank, [state])
                    yield
                bank, free = yield from slot(side_banks)
                for c in range(1, NC):
                    tok = slice(c * CHUNK, (c + 1) * CHUNK)
                    done = mm(bank[:, tok], Z[:, c - 1, :], Q_f[:, tok], True, True, [state, *free], signal=c == NC - 1)
                chunk_sets.put((P_T, Z), [done])
                yield
                later = slice(CHUNK, S)
                got = tt(y0[:, later], y0[:, later], bank[:, later], ALU.add, [done])
                side_banks.put(bank, [got])
                yield
                stat, free = yield from slot(side_banks)
                done = mm(stat[:, :], ones_head[:, :], y0, True, True, [got, *free], signal=True)
                yield
                centred = stt(y0, stat[:, :], -1.0 / HALF, y0, ALU.mult, ALU.add, [done])
                side_banks.put(stat, [centred])
                sq, free = yield from slot(scratch)
                got = act(sq[:, :], y0, ACT.Square, [centred, *free])
                yield
                stat, free = yield from slot(side_banks)
                done = mm(stat[:, :], ones_head[:, :], sq[:, :], True, True, [got, *free], signal=True)
                yield
                got_ln = act(sq[:, :], stat[:, :], ACT.Ln, [done], bias=EPSG, scale=1.0 / HALF)
                got = act(sq[:, :], sq[:, :], ACT.Exp, [got_ln], scale=-0.5)
                side_banks.put(stat, [got_ln])
                yield
                got = tt(y0, sq[:, :], y0, ALU.mult, [got])
                scratch.put(sq, [got])
                got = ts(y0, y0, column("lnx_g_2", f), column("lnx_b_2", f), ALU.mult, ALU.add, [got])
                got = tt(y0, y0, v_T[:, f, :], ALU.add, [got, features_of[f][6]])
                bank, free = yield from slot(side_banks)
                for n in range(2):
                    done = mm(bank[:, :], g_up[:, n, cols], gd_T[:, n, :], n == 0, n == 1, free, signal=n == 1)
                y_ready[f] = tt(y0, y0, bank[:, :], ALU.mult, [got, done])
                side_banks.put(bank, [y_ready[f]])

            for f in range(FW):
                spawn(features(f))
                spawn(chunk_half(f, 0))
                spawn(chunk_half(f, 1))
                spawn(states(f))
            finish_all()
            for _ in range(3):
                unit_banks.put(*side_banks.get())
            fence = q.latest()
        with ExitStack() as phase:
            y_b = pair(phase, "y_b", [P, FW, S])
            for f in range(FW):
                branch_tokens += split(y_b[0][:, f, :], y_b[1][:, f, :], k_T[:, f, :], [y_ready[f], *fence])

            def mix_part(part):
                return lambda k: (y_a[part][:, k, :] if k < FW else y_b[part][:, k - FW, :])

            class Mix:
                def __init__(self, part):
                    self.of = mix_part(part)

                def __getitem__(self, key):
                    return self.of(key[1])[key[0], key[2]]

            modulated_residual(2, "w_out_2", (Mix(0), Mix(1)), branch_tokens, token_projection)
        second.close()
        mixed_stack.close()
        fence = q.latest()


        for t in range(TT):
            x_ready[t] = normalise_rows(x_rows[t], D, EPS5, [x_ready[t]])
        with ExitStack() as phase:
            h3_T = pair(phase, "h3_T", [P, KT, S])
            hidden_T = pair(phase, "hidden_T", [P, FT, S])
            for engine in ("act", "dve", "pool"):
                q.wait(engine, fence)
            h3_ready = turn_scaled(x_rows, [[x_ready[t]] for t in range(TT)], *h3_T, lambda k: fold[:, 2, k:k + 1], TT,
                                   folded, lambda k: fold[:, 3, k:k + 1])
            gain_and_shift("ln1", "ln1_g", "ln1_b", h3_ready)

            def hidden(n):
                return hidden_T[0][:, n, :], hidden_T[1][:, n, :]

            f_ready = []
            for n in range(FT):
                bank, done = feature_unit(f"ffn_g.{n}", h3_T, waits=h3_ready)
                gate, free = scratch.get(tick)
                gated = act(gate[:, :], bank[:, :], ACT.Silu, [done, *free])
                unit_banks.put(bank, [gated])
                bank, done = feature_unit(f"ffn_u.{n}", h3_T)
                got = tt(gate[:, :], bank[:, :], gate[:, :], ALU.mult, [done, gated])
                unit_banks.put(bank, [got])
                both = split(*hidden(n), gate[:, :], [got, *fence])
                scratch.put(gate, both)
                f_ready.append(both)

            gates = gate_rows(5)
            held = [unit_banks.get(tick) for _ in range(3)] + [stat_bank.get(tick)] + [side_banks.get(tick) for _ in range(4)]
            for n in range(FT):
                u, (hi, lo), ready = take(f"ffn_out.{n}")
                f_hi, f_lo = hidden(n)
                for t in range(TT):
                    tok = slice(t * P, (t + 1) * P)
                    for half in range(2):
                        bank, free = held[2 * t + half]
                        cols = slice(half * 512, (half + 1) * 512)
                        last = n == FT - 1
                        done = mm3(bank[:, :], (f_hi[:, tok], f_lo[:, tok]), (hi[:, cols], lo[:, cols]), n == 0, last,
                                   [*ready, *f_ready[n], *free], signal=last or (t == TT - 1 and half == 1))
                        if last:
                            gate, gate_ready = gates[half]
                            product, free = scratch.get()
                            got = tt(product[:, :], bank[:, :], gate[:, :], ALU.mult, [done, gate_ready, *free])
                            x_ready[t] = stt(x_rows[t][:, cols], x_rows[t][:, cols], ALPHA, product[:, :], ALU.mult,
                                             ALU.add, [got, x_ready[t]])
                            scratch.put(product, [x_ready[t]])
                give_back(u, done)
            for gate, _ in gates:
                scratch.put(gate, [x_ready[-1]])
        for t in range(TT):
            x_ready[t] = normalise_rows(x_rows[t], D, EPS5, [x_ready[t]])
        gain_and_shift("ln2", "ln2_g", "ln2_b", [x_ready[-1]])
        sem_out = semaphore("out_stored")
        for t in range(TT):
            stored = load(out[t * P:(t + 1) * P, :], x_rows[t], sem_out, 16 * (t + 1), [x_ready[t]])
        q.wait("sync", [stored])

        block = whole.enter_context(nc.Block())

        @block.sync
        def _(eng):
            for step in q.steps["sync"]:
                step(eng)

        @block.scalar
        def _(eng):
            for step in q.steps["act"]:
                step(eng)

        @block.vector
        def _(eng):
            for step in q.steps["dve"]:
                step(eng)

        @block.gpsimd
        def _(eng):
            for step in q.steps["pool"]:
                step(eng)

        @block.tensor
        def _(eng):
            for step in q.steps["pe"]:
                step(eng)


def pack_weights(inputs):
    plan = unit_plan()
    packed = np.zeros((len(plan), P, UNIT), np.float32)
    for n, (_, array, kind, row, col) in enumerate(plan):
        w = np.asarray(inputs[array])[0]
        if kind == "F":
            part = w[:, col:col + P].reshape(KT, P, -1).transpose(1, 0, 2)
            packed[n].reshape(P, KT, P)[:, :, 0:part.shape[2]] = part
        elif kind == "T":
            packed[n] = w[row:row + 256, col:col + 512].reshape(2, P, 512).transpose(1, 0, 2).reshape(P, UNIT)
        else:
            packed[n] = w[row:row + P, :]
    return packed


def pack_columns(inputs):
    packed = np.zeros((N_COLUMNS, P), np.float32)
    for name, size in COLUMN_VECTORS:
        v = np.asarray(inputs[name]).reshape(-1)
        if size == HALF:
            v = np.concatenate([v, v])
        at = COLUMN_AT[name]
        packed.reshape(-1)[at * P:at * P + v.size] = v
    return np.ascontiguousarray(packed.T)


def kernel(**inputs):
    import concourse.bacc as bacc
    from concourse.bass_utils import run_bass_kernel_spmd

    arrays = {"weights": pack_weights(inputs), "columns": pack_columns(inputs)}

    def plain(name, source, shape):
        arrays[name] = np.ascontiguousarray(np.asarray(inputs[source]).reshape(shape))

    plain("x", "x", (S, D))
    plain("mem", "mem", (M, D))
    plain("w_ada", "w_ada_2", (D, 6 * D))
    for name in ("lambda_q1", "lambda_k1", "lambda_q2", "lambda_k2"):
        plain(name, name, (1, HALF))
    for name, size in (("emb_ln_g", D), ("emb_ln_b", D), ("ln1_g", D), ("ln1_b", D), ("ln2_g", D), ("ln2_b", D),
                       ("sg_ln_g", MIX), ("sg_ln_b", MIX), ("b_s", MIX)):
        plain(name, name + "_2", (1, size))
    plain("w_up", "w_up_2", (64, MIX))
    plain("a_up", "a_up_2", (64, MIX))
    plain("g_up", "g_up_2", (160, MIX))
    arrays["w_s"] = np.ascontiguousarray(np.asarray(inputs["w_s_2"])[0].transpose(2, 0, 1))
    nc = bacc.Bacc("TRN2", target_bir_lowering=False, num_devices=1)
    dram = {}
    for name, a in arrays.items():
        dram[name] = nc.dram_tensor("in_" + name, a.shape, FP32, kind="ExternalInput").ap()
    out = nc.dram_tensor("out", (S, D), FP32, kind="ExternalOutput").ap()
    build(nc, dram, out)
    result = run_bass_kernel_spmd(nc, [{"in_" + n: a for n, a in arrays.items()}], core_ids=[0])
    return result.results[0]["out"].reshape(1, S, D)
```
